# Optimizing a Trainium2 kernel written in Bass

```python
import jax, jax.numpy as jnp
from jax import lax
import numpy as np

D_MODEL = 1024
BATCH = 1
SEQ = 1024
DEPTH = 1

GRID_W = 64
CTX_LEN = 256
D_RNN = 512
RNN_HEADS = 8
RNN_HEAD_DIM = D_RNN // RNN_HEADS
RNN_CONV_W = 4
RNN_CONV_LEFT = 2
RG_C = 8.0
D_CONV = 512
CONV_GROUPS = 8
CONV_W = 3
D_CONV_H = D_CONV // 2
D_MIX = D_RNN + D_CONV
D_IN = 2 * D_RNN + 3 * D_CONV
N_GROUPS = 4
EXPERTS_PER_GROUP = 8
N_EXPERTS = N_GROUPS * EXPERTS_PER_GROUP
TOP_K = 2
D_EXPERT = 512
MOE_BLOCK = 128
NORM_EPS = 1e-6

kernel_name = "hybrid_rglru_shortconv_hiermoe_dit"

def rmsnorm(x, g):
    xf = x.astype(jnp.float32)
    y = xf * lax.rsqrt(jnp.mean(xf * xf, axis=-1, keepdims=True) + NORM_EPS)
    return (y * g.astype(jnp.float32)).astype(x.dtype)

def shift_conv(x, w, axis, left):
    k_w = w.shape[0]
    pad = [(0, 0)] * x.ndim
    pad[axis] = (left, k_w - 1 - left)
    xp = jnp.pad(x, pad)
    n = x.shape[axis]
    return sum(lax.slice_in_dim(xp, k, k + n, axis=axis) * w[k] for k in range(k_w))

def grid_short_conv(u, w, rows):
    bn, n, ch = u.shape
    ug = u.reshape(bn, rows, GRID_W, ch)
    uh = shift_conv(ug[..., :D_CONV_H], w[:, :D_CONV_H], axis=2, left=1)
    uv = shift_conv(ug[..., D_CONV_H:], w[:, D_CONV_H:], axis=1, left=1)
    return jnp.concatenate([uh, uv], axis=-1).reshape(bn, n, ch)

def rglru_coeffs(xc, wa, ba, wx, bx, lam):
    bn, n, _ = xc.shape
    xh = xc.reshape(bn, n, RNN_HEADS, RNN_HEAD_DIM)
    r = jax.nn.sigmoid(jnp.einsum('blhi,hij->blhj', xh, wa).reshape(bn, n, D_RNN) + ba)
    i = jax.nn.sigmoid(jnp.einsum('blhi,hij->blhj', xh, wx).reshape(bn, n, D_RNN) + bx)
    log_a = (-RG_C * r.astype(jnp.float32)) * jax.nn.softplus(-lam.astype(jnp.float32))
    a = jnp.exp(log_a)
    b = jnp.sqrt(-jnp.expm1(2.0 * log_a)) * (i * xc).astype(jnp.float32)
    return a, b

def _combine(e1, e2):
    a1, b1 = e1
    a2, b2 = e2
    return a1 * a2, a2 * b1 + b2

def linear_scan(a, b, h0, reverse):
    a_cum, h = lax.associative_scan(_combine, (a, b), axis=1, reverse=reverse)
    return h + a_cum * h0[:, None]

def hier_moe(xt, wg, bg, we, be, w_gate, w_up, w_down):
    t_n, d = xt.shape
    xf = xt.astype(jnp.float32)
    g_logits = xf @ wg.astype(jnp.float32) + bg.astype(jnp.float32)
    p_group = jax.nn.softmax(g_logits, axis=-1)
    grp = jnp.argmax(g_logits, axis=-1)
    p_g = jnp.max(p_group, axis=-1, keepdims=True)
    e_logits = (xf @ we.astype(jnp.float32) + be.astype(jnp.float32)).reshape(t_n, N_GROUPS, EXPERTS_PER_GROUP)
    e_in_grp = e_logits[jnp.arange(t_n), grp]
    top_p, top_local = lax.top_k(jax.nn.softmax(e_in_grp, axis=-1), TOP_K)
    gates = p_g * top_p / jnp.sum(top_p, axis=-1, keepdims=True)
    top_e = grp[:, None] * EXPERTS_PER_GROUP + top_local

    n_assign = t_n * TOP_K
    n_blocks = (n_assign + N_EXPERTS * (MOE_BLOCK - 1) + MOE_BLOCK - 1) // MOE_BLOCK
    flat_e = top_e.reshape(n_assign).astype(jnp.int32)
    order = jnp.argsort(flat_e)
    sorted_e = flat_e[order]
    counts = jnp.bincount(flat_e, length=N_EXPERTS)
    starts = jnp.cumsum(counts) - counts
    pcounts = (counts + MOE_BLOCK - 1) // MOE_BLOCK * MOE_BLOCK
    pends = jnp.cumsum(pcounts)
    pstarts = pends - pcounts
    dest = pstarts[sorted_e] + jnp.arange(n_assign) - starts[sorted_e]
    slot_tok = jnp.full((n_blocks * MOE_BLOCK,), t_n, jnp.int32).at[dest].set((order // TOP_K).astype(jnp.int32))
    x_pad = jnp.concatenate([xt, jnp.zeros((1, d), xt.dtype)], axis=0)
    xb = x_pad[slot_tok].reshape(n_blocks, MOE_BLOCK, d)
    block_e = jnp.minimum(jnp.sum(jnp.arange(n_blocks)[:, None] * MOE_BLOCK >= pends[None, :], axis=1), N_EXPERTS - 1)

    def run_block(args):
        xblk, e = args
        return (jax.nn.silu(xblk @ w_gate[e]) * (xblk @ w_up[e])) @ w_down[e]

    yb = lax.map(run_block, (xb, block_e)).reshape(n_blocks * MOE_BLOCK, d)
    y_assign = jnp.zeros((n_assign, d), yb.dtype).at[order].set(yb[dest])
    return jnp.einsum('tkd,tk->td', y_assign.reshape(t_n, TOP_K, d), gates.astype(yb.dtype))

def block(x, ctx_s, c, c_ctx, rows, last, ada_w, ada_b, norm1_g, norm2_g, w_in, rnn_conv_w, rnn_conv_b,
          rg_wa, rg_ba, rg_wx, rg_bx, rg_lambda, sc_conv_w, w_out, router_group_w, router_group_b,
          router_exp_w, router_exp_b, exp_w_gate, exp_w_up, exp_w_down):
    bn = x.shape[0]
    d = x.shape[-1]
    mod = jax.nn.silu(c) @ ada_w + ada_b
    sh1, sc1, g1, sh2, sc2, g2 = [m[:, None] for m in jnp.split(mod, 6, axis=-1)]
    mod_c = jax.nn.silu(c_ctx) @ ada_w + ada_b
    csh1, csc1, cg1, csh2, csc2, cg2 = jnp.split(mod_c, 6, axis=-1)

    splits = [D_RNN, 2 * D_RNN, 2 * D_RNN + D_CONV, 2 * D_RNN + 2 * D_CONV]
    h_lat = rmsnorm(x, norm1_g) * (1 + sc1) + sh1
    h_ctx = rmsnorm(ctx_s, norm1_g) * (1 + csc1) + csh1
    xr_l, gr_l, v_l, bgt_l, cgt_l = jnp.split(h_lat @ w_in, splits, axis=-1)
    xr_c, gr_c, v_c, bgt_c, cgt_c = jnp.split(h_ctx @ w_in, splits, axis=-1)

    xc_l = shift_conv(xr_l, rnn_conv_w, 1, RNN_CONV_LEFT) + rnn_conv_b
    xc_c = shift_conv(xr_c, rnn_conv_w, 1, RNN_CONV_LEFT) + rnn_conv_b
    hsum_l = jnp.zeros(xr_l.shape, jnp.float32)
    hsum_c = jnp.zeros(xr_c.shape, jnp.float32)
    for di, reverse in enumerate((False, True)):
        a_c, b_c = rglru_coeffs(xc_c, rg_wa[di], rg_ba[di], rg_wx[di], rg_bx[di], rg_lambda[di])
        h_c = linear_scan(a_c, b_c, jnp.zeros((bn, D_RNN), jnp.float32), reverse)
        h0 = h_c[:, 0] if reverse else h_c[:, -1]
        a_l, b_l = rglru_coeffs(xc_l, rg_wa[di], rg_ba[di], rg_wx[di], rg_bx[di], rg_lambda[di])
        hsum_l = hsum_l + linear_scan(a_l, b_l, h0, reverse)
        if not last:
            hsum_c = hsum_c + h_c

    y_rnn_l = jax.nn.gelu(gr_l, approximate=True) * hsum_l.astype(x.dtype)
    y_conv_l = bgt_l * grid_short_conv(cgt_l * v_l, sc_conv_w, rows)
    x = x + g1 * (jnp.concatenate([y_rnn_l, y_conv_l], axis=-1) @ w_out)
    if not last:
        y_rnn_c = jax.nn.gelu(gr_c, approximate=True) * hsum_c.astype(ctx_s.dtype)
        y_conv_c = bgt_c * shift_conv(cgt_c * v_c, sc_conv_w, 1, 1)
        ctx_s = ctx_s + cg1 * (jnp.concatenate([y_rnn_c, y_conv_c], axis=-1) @ w_out)

    m_l = (rmsnorm(x, norm2_g) * (1 + sc2) + sh2).reshape(-1, d)
    moe_args = (router_group_w, router_group_b, router_exp_w, router_exp_b, exp_w_gate, exp_w_up, exp_w_down)
    if last:
        x = x + g2 * hier_moe(m_l, *moe_args).reshape(x.shape)
        return x, None
    m_c = (rmsnorm(ctx_s, norm2_g) * (1 + csc2) + csh2).reshape(-1, d)
    n_ctx_tok = m_c.shape[0]
    y_all = hier_moe(jnp.concatenate([m_c, m_l], axis=0), *moe_args)
    ctx_s = ctx_s + cg2 * y_all[:n_ctx_tok].reshape(ctx_s.shape)
    x = x + g2 * y_all[n_ctx_tok:].reshape(x.shape)
    return x, ctx_s

def setup_inputs(seed: int = 0) -> dict:
    key = jax.random.key(seed)
    ks = jax.random.split(key, 32)
    f32 = jnp.float32
    nrm = lambda k, shape, s: jax.random.normal(k, shape, f32) * s
    a0 = jax.random.uniform(ks[12], (DEPTH, 2, D_RNN), f32, minval=0.9, maxval=0.999)
    return {
        "x": nrm(ks[0], (BATCH, SEQ, D_MODEL), 1.0),
        "c": nrm(ks[1], (BATCH, D_MODEL), 1.0),
        "ctx": nrm(ks[2], (BATCH, CTX_LEN, D_MODEL), 1.0),
        "c_ctx": nrm(ks[3], (D_MODEL,), 1.0),
        "ada_w": nrm(ks[4], (DEPTH, D_MODEL, 6 * D_MODEL), 0.5 * D_MODEL ** -0.5),
        "ada_b": nrm(ks[5], (DEPTH, 6 * D_MODEL), 0.01),
        "norm1_g": 1.0 + nrm(ks[6], (DEPTH, D_MODEL), 0.02),
        "norm2_g": 1.0 + nrm(ks[7], (DEPTH, D_MODEL), 0.02),
        "w_in": nrm(ks[8], (DEPTH, D_MODEL, D_IN), D_MODEL ** -0.5),
        "rnn_conv_w": nrm(ks[9], (DEPTH, RNN_CONV_W, D_RNN), RNN_CONV_W ** -0.5),
        "rnn_conv_b": nrm(ks[10], (DEPTH, D_RNN), 0.01),
        "rg_wa": nrm(ks[11], (DEPTH, 2, RNN_HEADS, RNN_HEAD_DIM, RNN_HEAD_DIM), RNN_HEAD_DIM ** -0.5),
        "rg_ba": nrm(ks[13], (DEPTH, 2, D_RNN), 0.01),
        "rg_wx": nrm(ks[14], (DEPTH, 2, RNN_HEADS, RNN_HEAD_DIM, RNN_HEAD_DIM), RNN_HEAD_DIM ** -0.5),
        "rg_bx": nrm(ks[15], (DEPTH, 2, D_RNN), 0.01),
        "rg_lambda": jnp.log(a0) - jnp.log1p(-a0),
        "sc_conv_w": nrm(ks[16], (DEPTH, CONV_W, D_CONV), CONV_W ** -0.5),
        "w_out": nrm(ks[17], (DEPTH, D_MIX, D_MODEL), D_MIX ** -0.5),
        "router_group_w": nrm(ks[18], (DEPTH, D_MODEL, N_GROUPS), D_MODEL ** -0.5),
        "router_group_b": nrm(ks[19], (DEPTH, N_GROUPS), 0.01),
        "router_exp_w": nrm(ks[20], (DEPTH, D_MODEL, N_EXPERTS), D_MODEL ** -0.5),
        "router_exp_b": nrm(ks[21], (DEPTH, N_EXPERTS), 0.01),
        "exp_w_gate": nrm(ks[22], (DEPTH, N_EXPERTS, D_MODEL, D_EXPERT), D_MODEL ** -0.5),
        "exp_w_up": nrm(ks[23], (DEPTH, N_EXPERTS, D_MODEL, D_EXPERT), D_MODEL ** -0.5),
        "exp_w_down": nrm(ks[24], (DEPTH, N_EXPERTS, D_EXPERT, D_MODEL), D_EXPERT ** -0.5),
        "final_norm_g": 1.0 + nrm(ks[25], (D_MODEL,), 0.02),
    }

def reference(x, c, ctx, c_ctx, ada_w, ada_b, norm1_g, norm2_g, w_in, rnn_conv_w, rnn_conv_b,
              rg_wa, rg_ba, rg_wx, rg_bx, rg_lambda, sc_conv_w, w_out, router_group_w, router_group_b,
              router_exp_w, router_exp_b, exp_w_gate, exp_w_up, exp_w_down, final_norm_g):
    rows = x.shape[1] // GRID_W
    ctx_s = ctx
    for l in range(DEPTH):
        x, ctx_s = block(x, ctx_s, c, c_ctx, rows, l == DEPTH - 1,
                         ada_w[l], ada_b[l], norm1_g[l], norm2_g[l], w_in[l], rnn_conv_w[l], rnn_conv_b[l],
                         rg_wa[l], rg_ba[l], rg_wx[l], rg_bx[l], rg_lambda[l], sc_conv_w[l], w_out[l],
                         router_group_w[l], router_group_b[l], router_exp_w[l], router_exp_b[l],
                         exp_w_gate[l], exp_w_up[l], exp_w_down[l])
    return rmsnorm(x, final_norm_g)


_drawn_inputs = setup_inputs


def setup_inputs(seed=0):
    import zlib

    import numpy as np

    out = dict(_drawn_inputs(seed))
    spreads = {}
    factors = {'ctx': 27.915,
     'ada_b': 2.925,
     'norm1_g': 4.461,
     'norm2_g': 15.455,
     'rnn_conv_b': 25.646,
     'rg_ba': 64.0,
     'rg_bx': 64.0,
     'router_group_b': 38.181,
     'router_exp_b': 64.0,
     'final_norm_g': 7.623,
     'c_ctx': 7.084}
    for name, (base, spread) in spreads.items():
        noise = np.random.default_rng([zlib.crc32(name.encode()), seed]).standard_normal(out[name].shape)
        drawn = base * np.exp(spread * noise) if base else spread * noise
        out[name] = __import__('jax').numpy.asarray(drawn.astype(out[name].dtype))
    for name, factor in factors.items():
        out[name] = (out[name] * factor).astype(out[name].dtype)
    return out
```

```python
from contextlib import ExitStack

import numpy as np
import concourse.bass as bass
from concourse import mybir

F32 = mybir.dt.float32
F32R = mybir.dt.float32r
I32 = mybir.dt.int32
U32 = mybir.dt.uint32
ACT = mybir.ActivationFunctionType
ALU = mybir.AluOpType
AX = mybir.AxisListType.X

P = 128
D = 1024
KT = D // P
SEQ, CTX = 1024, 256
NT = SEQ // P
NTC = NT + CTX // P
GRID_W = 64
TAPS, CTAPS = 4, 3
CT = 512 // P
RG_C = 8.0
EPS = 1e-6
NG, EPG, NE = 4, 8, 32
FF = 512
FT = FF // P
TOPK = 2
NOVF = (TOPK * SEQ) // P
NB = NE + NOVF + 2
NONE = 4096
LAT = CTX + 3
XC = LAT + SEQ
XR = XC + TAPS - 1
PIECE = 256
RING = 3
RAW, SPLIT = 6, 4
CHUNK = 4096
UNIT = CHUNK // 2

ROWS = {}
_at = 0
for _name, _n in (("conv_w", TAPS * CT), ("conv_b", CT), ("ba", 2 * CT), ("bx", 2 * CT), ("lam", 2 * CT),
                  ("sc_w", CTAPS * CT), ("g1n", KT), ("ada_b", 2 * KT), ("c", 2 * KT)):
    ROWS[_name] = (_at, _n)
    _at += _n
NROWS = _at


def order(text):
    steps = []
    for word in text.split():
        name = word.rstrip("0123456789.")
        steps.append((name, *(int(n) for n in word[len(name):].split("."))))
    return steps


ACT_ORDER = order("""
    post0 split2 post1 split3 post2 ri0.0 split4 post3 root0.0 ri0.1 root0.1 split5 yhi0 post4 ri1.0 root1.0 split6
    split7 ri1.1 root1.1 yhi1 post5 post6 split8 ri2.0 root2.0 post7 split9 ri2.1 root2.1 yhi2 post8 split10 ri3.0
    root3.0 ri3.1 root3.1 yhi3 post9 split11 split12 split13 yhi4 split14 yhi5 split15 post14 split16 post15 split17
    split18 split19 yhi6 yhi7""")
DVE_ORDER = order("""
    conv0 split2 split3 split4 scan0.0 scan0.1 split5 conv1 yrnn0 ylo0 scan1.0 split6 split7 scan1.1 conv2 yrnn1 ylo1
    split8 scan2.0 split9 scan2.1 conv3 yrnn2 ylo2 ada0 split10 scan3.0 scan3.1 yrnn3 ylo3 ada1 ada2 split11 v10 ada3
    split12 v11 ada4 ada5 split13 b12 ylo4 row0 row1 ada6 split14 b13 ylo5 row2 row3 ada7 split15 row4 row5 ada8
    split16 row6 row7 ada9 ada10 split17 v16 row8 row9 ada11 split18 v17 row10 row11 ada12 ada13 split19 b18 ylo6
    row12 row13 ada14 ada15 b19 ylo7 row14 row15""")


class Own:

    def __init__(self, eng, sem):
        self.eng, self.sem, self.n = eng, sem, 0

    def did(self, instruction):
        instruction.then_inc(self.sem, 1)
        self.n = self.n + 1

    def wait(self):
        if self.n:
            self.eng.wait_ge(self.sem, self.n)


class Block:

    def __init__(self, n, half, par):
        self.n, self.half, self.par = n, half, par


class Chunk:

    def __init__(self, n, slot, turn):
        self.n, self.slot, self.turn = n, slot, turn


def layer(nc, A, out):
    ctx = ExitStack()
    with ctx:
        def sem(name):
            return ctx.enter_context(nc.semaphore(name))

        top = {"at": (nc.sbuf_base + 63) // 64 * 64}

        def place(name, shape, dt, at):
            return nc.alloc_sbuf_tensor_at(name, shape, dt, offset=at)

        def const(name, shape, dt=F32):
            n = int(np.prod(shape[1:])) * 4
            t = place(name, shape, dt, top["at"])
            top["at"] += (n + 31) // 32 * 32
            return t

        K = 1024
        ident = const("ident", [P, P])
        ones = const("ones", [P, P])
        tri = const("tri", [P, P])
        iota = const("iota", [P, P])
        prm = const("prm", [P, P])
        prmT = const("prmT", [P, NROWS])
        silu_c = const("silu_c", [P, 2 * KT])
        mod_a = const("mod_a", [P, 2, KT])
        mod_s = const("mod_s", [P, 2, KT])
        q8 = const("q8", [P, 2 * CT])
        nq8 = const("nq8", [P, 2 * CT])
        spt = const("spt", [P, 5, 2 * CT])
        ssq = const("ssq", [P, 16])
        std = const("std", [P, 16])
        rstd = const("rstd", [P, 16])
        w_route = const("w_route", [P, KT, NG + NE])
        b_route = const("b_route", [1, NG + NE])
        adab2 = const("adab2", [16, PIECE])
        eps = const("eps", [P, 1])
        marks = const("marks", [P, 4])
        ones_e = const("ones_e", [P, NE])
        tok_id = const("tok_id", [P, TOPK, NT])
        tok_tab = const("tok_tab", [P, NB + 1], I32)
        id_tab = const("id_tab", [P, NB + 1], I32)
        gate_tab = const("gate_tab", [P, NB])
        ovf_exp = const("ovf_exp", [P, NOVF], I32)
        n_ovf = const("n_ovf", [P, 1], I32)
        tok_now = [const(f"tok_now{i}", [P, 1], I32) for i in range(2)]
        id_now = [const(f"id_now{i}", [P, 1], I32) for i in range(2)]
        gate_now = [const(f"gate_now{i}", [P, 1]) for i in range(2)]
        aH = (top["at"] + 63) // 64 * 64
        aY = aH + 80 * K
        aT = aY + 64 * K
        aWR = aT + 16 * K
        aWS = aWR + 24 * K
        assert aWS + 16 * K <= nc.sbuf_usable_end, (aWS + 16 * K, nc.sbuf_usable_end)

        h_hi = place("h_hi", [P, KT, SEQ], F32R, aH)
        h_lo = place("h_lo", [P, KT, SEQ], F32R, aH + 32 * K)
        hc_hi = place("hc_hi", [P, KT, CTX], F32R, aH + 64 * K)
        hc_lo = place("hc_lo", [P, KT, CTX], F32R, aH + 72 * K)
        x_all = place("x_all", [P, NTC, D], F32, aY)
        h_tmp = place("h_tmp", [P, 2, 512], F32, aT)
        piece = [place(f"piece{i}", [P, KT, PIECE], F32, aWR + 8 * K * i) for i in range(RING)]
        ws_hi = [place(f"ws_hi{i}", [P, KT, P], F32R, aWS + 8 * K * i) for i in range(2)]
        ws_lo = [place(f"ws_lo{i}", [P, KT, P], F32R, aWS + 8 * K * i + 4 * K) for i in range(2)]
        y_hi = [place(f"y_hi{i}", [P, SEQ], F32R, aY + 4 * K * i + (16 * K if i >= 4 else 0)) for i in range(8)]
        y_lo = [place(f"y_lo{i}", [P, SEQ], F32R, aY + 16 * K + 4 * K * i + (16 * K if i >= 4 else 0)) for i in range(8)]
        aR = aY + 32 * K
        gate_w = place("gate_w", [P, CT, 4, P], F32, aR)
        r_at = aR + 8 * K
        step = (XR * 4 + 31) // 32 * 32
        xr_pad = place("xr_pad", [P, XR], F32, r_at)
        xc = place("xc", [P, XC], F32, r_at + step)
        r_a = place("r_a", [P, XC], F32, r_at + 2 * step)
        t_s = place("t_s", [P, XC], F32, r_at + 3 * step)
        v_s = place("v_s", [P, XC], F32, r_at + 4 * step)
        i_h = [place(f"i_h{d}", [P, XC], F32, r_at + (5 + d) * step) for d in range(2)]
        r_end = r_at + 7 * step
        assert r_end <= aT + 12 * K
        gelu_g = [place("gelu_g0", [P, SEQ], F32, aY + 12 * K), place("gelu_g1", [P, SEQ], F32, aY + 28 * K)]
        conv_u = [place(f"conv_u{i}", [P, SEQ], F32, aT + 12 * K * (1 - i)) for i in range(2)]
        conv_y = [place(f"conv_y{i}", [P, SEQ], F32, aT + 4 * K + 4 * K * i) for i in range(2)]
        wo_hi = place("wo_hi", [P, KT, D], F32R, aH)
        wo_lo = place("wo_lo", [P, KT, D], F32R, aH + 32 * K)
        rows = place("rows", [P, 4, D], F32, aH + 64 * K)
        x_in = [place(f"x_in{i}", [P, D], F32, aWS + 8 * K * i) for i in range(2)]
        x1 = [place(f"x1_{i}", [P, D], F32, aWS + 8 * K * i + 4 * K) for i in range(2)]
        norm2 = place("norm2", [P, D], F32, aT + 4 * K)
        m_row = [place(f"m_row{i}", [P, D], F32, aT + 4 * K * i) for i in range(2)]
        mT = [place(f"mT{i}", [P, KT, P], F32, aT + 8 * K + 4 * K * i) for i in range(2)]
        slot_hot = place("slot_hot", [P, 16, P], F32, aWR + 16 * K)
        rt = {"at": aWS}

        def tmp(name, shape, dt=F32):
            t = place(name, shape, dt, rt["at"])
            rt["at"] += (int(np.prod(shape[1:])) * 4 + 31) // 32 * 32
            assert rt["at"] <= aWS + 16 * K
            return t

        logit = tmp("logit", [P, NT, NG + NE])
        g_pad = tmp("g_pad", [P, NT, 8])
        g_top = tmp("g_top", [P, NT, 8])
        g_idx = tmp("g_idx", [P, NT, 8], U32)
        e8 = tmp("e8", [P, NT, 8])
        e_top = tmp("e_top", [P, NT, 8])
        e_idx = tmp("e_idx", [P, NT, 8], U32)
        gi = tmp("gi", [P, NT])
        g_hot = tmp("g_hot", [P, NT, NG])
        xs = tmp("xs", [P, NT, 14])
        xe = tmp("xe", [P, NT, 14])
        dens = tmp("dens", [P, 4, NT])
        gates = tmp("gates", [P, TOPK, NT])
        e_k = tmp("e_k", [P, TOPK, NT])
        big = tmp("big", [P, NT, NE])
        hot = tmp("hot", [P, TOPK, NT, NE])
        hot_s = tmp("hot_s", [P, NT, NE])
        pre = tmp("pre", [P, NT + 1, NE])
        rank = tmp("rank", [P, TOPK, NT])
        rank_i = tmp("rank_i", [P, TOPK, NT], I32)
        bq_i = tmp("bq_i", [P, TOPK, NT], I32)
        s_i = tmp("s_i", [P, TOPK, NT], I32)
        bq = tmp("bq", [P, TOPK, NT])
        s_f = tmp("s_f", [P, TOPK, NT])
        ov_k = tmp("ov_k", [P, TOPK, NT])
        blk_k = tmp("blk_k", [P, TOPK, NT])
        cnt = tmp("cnt", [P, NE])
        cnt_i = tmp("cnt_i", [P, NE], I32)
        extra = tmp("extra", [P, NE])
        incl = tmp("incl", [P, NE])
        excl = tmp("excl", [P, NE])
        ov_f = tmp("ov_f", [P, NOVF])
        slots_f = tmp("slots_f", [P, 2, NB])
        slot_v = tmp("slot_v", [P, NB])
        blk_hot = place("blk_hot", [P, TOPK * NT, 2, NB], F32, aY)
        ovf_c = place("ovf_c", [P, NOVF, NE], F32, aY + 8 * K)
        raw_at = [aWR] + [aH + 16 * K * i for i in range(5)]
        raw = [place(f"raw{i}", [P, CHUNK], F32, raw_at[i]) for i in range(RAW)]
        w_hi = [place(f"w_hi{i}", [P, UNIT], F32R, aY + 16 * K * i) for i in range(SPLIT)]
        w_lo = [place(f"w_lo{i}", [P, UNIT], F32R, aY + 16 * K * i + 8 * K) for i in range(SPLIT)]
        xT_hi = place("xT_hi", [P, KT, P], F32R, aWS)
        xT_lo = place("xT_lo", [P, KT, P], F32R, aWS + 4 * K)
        s_act = place("s_act", [P, FF], F32, aWS + 8 * K)
        h_act = place("h_act", [P, FF], F32, aWS + 10 * K)
        hT_hi = place("hT_hi", [P, FT, P], F32R, aWS + 12 * K)
        hT_lo = place("hT_lo", [P, FT, P], F32R, aWS + 14 * K)
        x_e = [place(f"x_e{i}", [P, D], F32, aT + 4 * K * i) for i in range(2)]
        y_e = [place(f"y_e{i}", [P, D], F32, aT + 8 * K + 4 * K * i) for i in range(2)]
        fin = [place(f"fin{i}", [P, 4, D], F32, aH + 16 * K * i) for i in range(4)]
        fin_rows = place("fin_rows", [P, 2, D], F32, aWR)

        main = ctx.enter_context(nc.psum_tensor("main", [P, 2, 1024], F32))
        lat = ctx.enter_context(nc.psum_tensor("lat", [P, 2, 512], F32))
        b6 = ctx.enter_context(nc.psum_tensor("b6", [P, 512], F32))
        b7 = ctx.enter_context(nc.psum_tensor("b7", [P, 512], F32))

        x1_d = nc.dram_tensor("x1_d", [SEQ, D], F32, kind="Internal").ap()
        m_d = nc.dram_tensor("m_d", [SEQ, D], F32, kind="Internal").ap()
        y_d = nc.dram_tensor("y_d", [TOPK * SEQ, D], F32, kind="Internal").ap()
        g2_d = nc.dram_tensor("g2_d", [1, D], F32, kind="Internal").ap()

        names = """params_in x0_in x1_in xc_in gate_w_in route_in norm2_in adab2_in
            act_own dve_own pool_own consts_set gatew_zero params_turned params_set silu_set lam_exp lam_ln lam_w coef_set
            ada1_used mod_done mod_set sq_done std_set xs_set turned unit_h unit_hi unit_lo
            piece_used m_hi m_lo main_done free0 free1 ctx_free pads_set xr_set xc_set gate_done gate_free
            ri_set tanh_set exp_set s2_set s_set scan_done gelu_set y_set yhi_set ylo_set u_set
            acc_set bc_done row_set g2_out wo_hi_s wo_lo_s
            x_in0 x_in1 x1_set x1_out0 x1_out1 m_set m_out0 m_out1 mturn_done mT_set logit_done logit_set
            rexp_in rexp_set hot_set cum_done tabs_in tabs_done tabs_set
            ex_tok ex_id ex_gate gath0 gath1 scat0 scat1 tx_done xh_set xl_set gate_mm up_mm silu_e h_set th_done hh_set hl_set
            down_mm y_out unit_used hi_done lo_done
            fx0 fx1 fx2 fx3 frow_in fsum fsq fstd fout fo0 fo1 fo2 fo3 moe_done_a moe_done_p""".split()
        S = {n: sem(n) for n in names}
        ring_in = [sem(f"ring_in{i}") for i in range(RING)]
        raw_in = [sem(f"raw_in{i}") for i in range(RAW)]

        ada = A["ada_w"][0].rearrange("(j p) n -> p j n", p=P)
        w_in = A["w_in"][0].rearrange("(j p) n -> p j n", p=P)
        w_out = A["w_out"][0].rearrange("(j p) n -> p j n", p=P)
        N_ADA1 = 2 * D // PIECE
        kinds = [("ada1", i) for i in range(N_ADA1)] + [("w", 0), ("w", 1), ("w", 2), ("w", 3)]
        a2 = 0
        for half in range(2):
            for k, n_a in ((0, 3), (1, 3), (2, 2)):
                kinds.append(("w", 4 + 3 * half + k))
                kinds += [("ada2", a2 + i) for i in range(n_a)]
                a2 += n_a
        N_ADA2 = a2
        kinds += [("wo", i) for i in range(4)]
        assert N_ADA2 * PIECE == 4 * D
        piece_no = {k: n for n, k in enumerate(kinds)}
        v0, bgt0, cgt0 = 1024, 1536, 2048
        w_col = [0, 512, PIECE, 512 + PIECE]
        for half in range(2):
            w_col += [cgt0 + PIECE * half, v0 + PIECE * half, bgt0 + PIECE * half]
        what = [("xr", 0), ("xr", 1), ("gr", 0), ("gr", 1), ("xr", 2), ("xr", 3), ("gr", 2), ("gr", 3)]
        for half in range(2):
            for k in ("cg", "v", "b"):
                what += [(k, 2 * half), (k, 2 * half + 1)]
        N_MAIN = len(what)
        what_index = {w: n for n, w in enumerate(what)}

        def piece_src(kind, i):
            if kind == "ada1":
                return ada[:, :, PIECE * i:PIECE * (i + 1)]
            if kind == "ada2":
                return ada[:, :, 2 * D + PIECE * i:2 * D + PIECE * (i + 1)]
            if kind == "w":
                return w_in[:, :, w_col[i]:w_col[i] + PIECE]
            return w_out[:, 2 * i:2 * i + 2, :]

        def piece_dst(n):
            kind, _ = kinds[n]
            t = piece[n % RING]
            return t[:] if kind != "wo" else t[:].rearrange("p j n -> p (j n)").rearrange("p (j n) -> p j n", j=2)

        def piece_wait(eng, n):
            eng.wait_ge(ring_in[n % RING], 16 * (n // RING + 1))

        def col(name, i):
            at, n = ROWS[name]
            assert i < n
            return prmT[:, at + i:at + i + 1]

        def cols(name):
            at, n = ROWS[name]
            return prmT[:, at:at + n]

        free = [S["free0"], S["free1"]]
        groups = [(0, 4, 0), (4, 4, 0), (8, 2, 1)]
        units = [(g, j) for g in range(3) for j in range(KT)]

        def bank(u):
            return main[:, (u % 4) // 2, 512 * (u % 2):512 * (u % 2) + 512]

        exp_w = {"g": A["exp_w_gate"].rearrange("l e (p j) n -> (l e) p (j n)", p=P),
                 "u": A["exp_w_up"].rearrange("l e (p j) n -> (l e) p (j n)", p=P),
                 "d": A["exp_w_down"].rearrange("l e (p j) n -> (l e) p (j n)", p=P)}

        def step_plan(i, k):
            b = Block(2 * i + 3 + k, i + (3 + k) // 2, (3 + k) % 2)
            cs = [Chunk(6 * i + 8 + 3 * k + c, (8 + 3 * k + c) % RAW, i + (8 + 3 * k + c) // RAW) for c in range(3)]
            return b, cs

        def plain(b):
            c0 = 3 * b - 1 if b else 0
            return Block(b, b // 2, b % 2), [Chunk(c0 + c, (c0 + c) % RAW, (c0 + c) // RAW) for c in range(3)]

        def before(b):
            return Block(b.n - 1, b.half - 1 + b.par, 1 - b.par)

        def after(b):
            return Block(b.n + 1, b.half + b.par, 1 - b.par)

        LOOPS = (NE - 4) // 2
        LAST = Chunk(3 * NE - 1, (3 * NE - 1) % RAW, (3 * NE - 1) // RAW)

        def pair_plan(i):
            base = 3 * NE
            return [(Block(NE + 2 * i + k, NE // 2 + i, k),
                     [Chunk(base + 6 * i + 3 * k + c, (3 * k + c) % RAW, base // RAW + i) for c in range(3)])
                    for k in range(2)]

        gath, scat = [S["gath0"], S["gath1"]], [S["scat0"], S["scat1"]]

        block = ctx.enter_context(nc.Block())

        @block.sync
        def _(sp):
            def rows_in(name, src):
                at, n = ROWS[name]
                sp.dma_start(prm[at:at + n, :], src).then_inc(S["params_in"], 16)

            rows_in("conv_w", A["rnn_conv_w"][0].rearrange("k (c p) -> (k c) p", p=P))
            rows_in("conv_b", A["rnn_conv_b"][0].rearrange("(c p) -> c p", p=P))
            rows_in("ba", A["rg_ba"][0].rearrange("d (c p) -> (d c) p", p=P))
            rows_in("bx", A["rg_bx"][0].rearrange("d (c p) -> (d c) p", p=P))
            rows_in("lam", A["rg_lambda"][0].rearrange("d (c p) -> (d c) p", p=P))
            rows_in("sc_w", A["sc_conv_w"][0].rearrange("k (c p) -> (k c) p", p=P))
            rows_in("g1n", A["norm1_g"][0].rearrange("(c p) -> c p", p=P))
            rows_in("ada_b", A["ada_b"][0, 0:2 * D].rearrange("(c p) -> c p", p=P))
            at = ROWS["c"][0]
            sp.dma_start(prm[at:at + KT, :], A["c"][0].rearrange("(c p) -> c p", p=P)).then_inc(S["params_in"], 16)
            sp.dma_start(prm[at + KT:at + 2 * KT, :], A["c_ctx"].rearrange("(c p) -> c p", p=P)).then_inc(S["params_in"], 16)
            x_rows = A["x"][0].rearrange("(t p) d -> p t d", p=P)

            def load_piece(n):
                if n >= RING:
                    m = n - RING
                    if m < N_ADA1:
                        sp.wait_ge(S["ada1_used"], m + 1)
                    else:
                        sp.wait_ge(S["piece_used"], m - N_ADA1 + 1)
                sp.dma_start(piece_dst(n), piece_src(*kinds[n])).then_inc(ring_in[n % RING], 16)

            sp.dma_start(x_all[:, 0:4, :], x_rows[:, 0:4, :]).then_inc(S["x0_in"], 16)
            for n in range(N_ADA1 + 1):
                load_piece(n)
            sp.dma_start(x_all[:, 4:8, :], x_rows[:, 4:8, :]).then_inc(S["x1_in"], 16)
            sp.dma_start(x_all[:, 8:10, :], A["ctx"][0].rearrange("(t p) d -> p t d", p=P)).then_inc(S["xc_in"], 16)
            for n in range(N_ADA1 + 1, N_ADA1 + 2):
                load_piece(n)
            sp.wait_ge(S["gatew_zero"], 1)
            for d in range(2):
                for kind, src in ((0, A["rg_wa"]), (1, A["rg_wx"])):
                    for e in range(2):
                        dst = gate_w[64 * e:64 * e + 64, :, 2 * d + kind, 64 * e:64 * e + 64]
                        sp.dma_start(dst, src[0, d].rearrange("(c e) i j -> e i c j", e=2)[e]).then_inc(S["gate_w_in"], 16)
            sp.dma_start(w_route[:, :, 0:NG], A["router_group_w"][0].rearrange("(j p) n -> p j n", p=P)).then_inc(S["route_in"], 16)
            sp.dma_start(w_route[:, :, NG:NG + NE], A["router_exp_w"][0].rearrange("(j p) n -> p j n", p=P)).then_inc(S["route_in"], 16)
            sp.dma_start(b_route[:, 0:NG], A["router_group_b"]).then_inc(S["route_in"], 16)
            sp.dma_start(b_route[:, NG:NG + NE], A["router_exp_b"]).then_inc(S["route_in"], 16)
            sp.dma_start(adab2[:], A["ada_b"][0, 2 * D:6 * D].rearrange("(a n) -> a n", n=PIECE)).then_inc(S["adab2_in"], 16)
            for n in range(N_ADA1 + 2, piece_no[("w", 4)]):
                load_piece(n)
            for n in range(piece_no[("w", 4)], len(kinds)):
                load_piece(n)
            sp.wait_ge(S["ylo_set"], KT)
            sp.dma_start(norm2[:], A["norm2_g"].to_broadcast([P, D])).then_inc(S["norm2_in"], 16)
            x_in_s, x1_out, m_out = [S["x_in0"], S["x_in1"]], [S["x1_out0"], S["x1_out1"]], [S["m_out0"], S["m_out1"]]
            sp.wait_ge(S["main_done"], N_MAIN)
            for t in range(2):
                sp.dma_start(x_in[t][:], A["x"][0, P * t:P * t + P, :]).then_inc(x_in_s[t], 16)
            sp.wait_ge(S["piece_used"], len(kinds) - N_ADA1)

            def load_chunk(c, which, e, guard):
                if guard:
                    sp.wait_ge(S["lo_done"], 2 * (c.n - RAW) + 2)
                src = exp_w[which]
                src = src[e] if isinstance(e, int) else src[bass.ds(e, 1)].rearrange("a p f -> (a p) f")
                sp.dma_start(raw[c.slot][:], src).then_inc(raw_in[c.slot], 16)

            sp.dma_start(raw[0][:], exp_w["g"][0]).then_inc(raw_in[0], 16)
            sp.wait_ge(S["row_set"], N_ADA2)
            sp.dma_start(g2_d, rows[0:1, 3, :]).then_inc(S["g2_out"], 16)
            sp.wait_ge(S["g2_out"], 16)
            for t in range(NT):
                sp.wait_ge(S["x1_set"], t + 1)
                sp.dma_start(x1_d[P * t:P * t + P, :], x1[t % 2][:]).then_inc(x1_out[t % 2], 16)
                if t + 2 < NT:
                    sp.dma_start(x_in[t % 2][:], A["x"][0, P * (t + 2):P * (t + 3), :]).then_inc(x_in_s[t % 2], 16)
                sp.wait_ge(S["m_set"], t + 1)
                sp.dma_start(m_d[P * t:P * t + P, :], m_row[t % 2][:]).then_inc(m_out[t % 2], 16)
            sp.wait_ge(S["main_done"], N_MAIN + NT)
            first = [("g", 0), ("u", 0), ("g", 1), ("u", 1), ("d", 0), ("g", 2)]
            for c in range(1, RAW):
                sp.dma_start(raw[c][:], exp_w[first[c][0]][first[c][1]]).then_inc(raw_in[c], 16)
            _, cs = plain(2)
            load_chunk(cs[1], "u", 2, True)
            load_chunk(cs[2], "d", 1, True)
            with sp.Fori(0, LOOPS) as i:
                for k in range(2):
                    _, cs = step_plan(i, k)
                    load_chunk(cs[0], "g", 2 * i + 3 + k, True)
                    load_chunk(cs[1], "u", 2 * i + 3 + k, True)
                    load_chunk(cs[2], "d", 2 * i + 2 + k, True)
            _, cs = plain(NE - 1)
            load_chunk(cs[0], "g", NE - 1, True)
            load_chunk(cs[1], "u", NE - 1, True)
            load_chunk(cs[2], "d", NE - 2, True)
            load_chunk(LAST, "d", NE - 1, True)
            more = sp.value_load(n_ovf[0:1, 0:1], min_val=0, max_val=NOVF)
            with sp.Fori(0, NOVF // 2) as i:
                with sp.If(2 * i < more):
                    for k, (b, cs) in enumerate(pair_plan(i)):
                        e = sp.value_load(ovf_exp[0:1, bass.ds(2 * i + k, 1)], min_val=0, max_val=NE - 1)
                        for c, which in zip(cs, "gud"):
                            load_chunk(c, which, e, True)
                sp.nop()
            fx, fo = [S[f"fx{i}"] for i in range(4)], [S[f"fo{i}"] for i in range(4)]
            sp.wait_ge(S["moe_done_a"], 1)
            sp.wait_ge(S["moe_done_p"], 1)
            sp.dma_start(fin_rows[:, 0, :], g2_d.to_broadcast([P, D])).then_inc(S["frow_in"], 16)
            sp.dma_start(fin_rows[:, 1, :], A["final_norm_g"].rearrange("(a n) -> a n", a=1).to_broadcast([P, D])).then_inc(S["frow_in"], 16)
            y_rows = y_d.rearrange("(k t p) d -> t p k d", k=TOPK, p=P)
            out_rows = out[0].rearrange("(t p) d -> t p d", p=P)

            def fin_load(t):
                sp.dma_start(fin[t % 4][:, 0:2, :], y_rows[t]).then_inc(fx[t % 4], 16)
                sp.dma_start(fin[t % 4][:, 2, :], x1_d[P * t:P * t + P, :]).then_inc(fx[t % 4], 16)

            for t in range(4):
                fin_load(t)
            for t in range(NT):
                sp.wait_ge(S["fout"], t + 1)
                sp.dma_start(out_rows[t], fin[t % 4][:, 3, :]).then_inc(fo[t % 4], 16)
                if t + 4 < NT:
                    fin_load(t + 4)
            for i in range(4):
                sp.wait_ge(fo[i], 16 * (NT // 4))

        @block.gpsimd
        def _(pool):
            own = Own(pool, S["pool_own"])
            own.did(pool.memset(ident[:], 0.0))
            own.did(pool.memset(ones[:], 1.0))
            own.did(pool.memset(tri[:], 1.0))
            own.wait()
            own.did(pool.affine_select(out=ident[:], in_=ident[:], compare_op=ALU.not_equal, fill=1.0, base=0,
                                       pattern=[[-1, P]], channel_multiplier=1))
            own.did(pool.affine_select(out=tri[:], in_=tri[:], compare_op=ALU.is_gt, fill=0.0, base=0,
                                       pattern=[[1, P]], channel_multiplier=-1))
            own.did(pool.iota(iota[:], [[1, P]], base=0, channel_multiplier=0, allow_small_or_imprecise_dtypes=True))
            own.did(pool.iota(tok_id[:].rearrange("p k t -> p (k t)"), [[P, TOPK * NT]], base=1, channel_multiplier=1,
                              allow_small_or_imprecise_dtypes=True))
            own.wait()
            pool.memset(ones_e[:], 1.0).then_inc(S["consts_set"], 1)
            pool.wait_ge(S["turned"], len(units))
            pool.memset(gate_w[:], 0.0).then_inc(S["gatew_zero"], 1)
            pool.wait_ge(S["unit_lo"], len(units))
            pool.memset(xr_pad[:], 0.0).then_inc(S["pads_set"], 1)
            for t in (r_a, t_s, v_s, i_h[0], i_h[1]):
                pool.memset(t[:, CTX:LAT], 0.0).then_inc(S["pads_set"], 1)

            def gather(b, first):
                if not first:
                    pool.wait_ge(S["tx_done"], b.n - 1)
                if not (isinstance(b.n, int) and b.n < 2):
                    pool.wait_ge(gath[b.par], 16 * b.half)
                pool.tensor_copy(tok_now[b.par][:], tok_tab[:, bass.ds(b.n + 1, 1)]).then_inc(S["ex_tok"], 1)
                pool.wait_ge(S["tabs_set"], 1)
                pool.wait_ge(S["ex_tok"], b.n + 1)
                pool.indirect_dma_start(out=x_e[b.par][:], out_offset=None, in_=m_d,
                                        in_offset=bass.IndirectOffsetOnAxis(ap=tok_now[b.par][:].bitcast(U32), axis=0),
                                        bounds_check=SEQ - 1, oob_is_err=False).then_inc(gath[b.par], 16)

            def gate_col(b, first):
                if not first:
                    pool.wait_ge(S["y_out"], b.n - 1)
                pool.tensor_copy(gate_now[b.par][:], gate_tab[:, bass.ds(b.n, 1)]).then_inc(S["ex_gate"], 1)

            def scatter(b, first):
                if not first:
                    pool.wait_ge(scat[b.par], 16 * b.half)
                pool.tensor_copy(id_now[b.par][:], id_tab[:, bass.ds(b.n + 1, 1)]).then_inc(S["ex_id"], 1)
                pool.wait_ge(S["tabs_set"], 1)
                pool.wait_ge(S["ex_id"], b.n + 1)
                pool.wait_ge(S["y_out"], b.n + 1)
                pool.indirect_dma_start(out=y_d, out_offset=bass.IndirectOffsetOnAxis(ap=id_now[b.par][:].bitcast(U32), axis=0),
                                        in_=y_e[b.par][:], in_offset=None,
                                        bounds_check=TOPK * SEQ - 1, oob_is_err=False).then_inc(scat[b.par], 16)

            def blk(n):
                return Block(n, n // 2, n % 2)

            pool.wait_ge(S["tabs_set"], 1)
            pool.wait_ge(S["m_out0"], 16 * (NT // 2))
            pool.wait_ge(S["m_out1"], 16 * (NT // 2))
            pool.memset(x_e[0][:], 0.0).then_inc(S["pool_own"], 1)
            pool.memset(x_e[1][:], 0.0).then_inc(S["pool_own"], 1)
            own.n = own.n + 2
            own.wait()
            gather(blk(0), True)
            gather(blk(1), True)
            gate_col(blk(0), True)
            gather(blk(2), False)
            gate_col(blk(1), True)
            gather(blk(3), False)
            gate_col(blk(2), False)
            gather(blk(4), False)
            gather(blk(5), False)
            scatter(blk(0), True)
            gate_col(blk(3), False)
            scatter(blk(1), True)
            with pool.Fori(0, LOOPS) as i:
                for k in range(2):
                    gather(Block(2 * i + 6 + k, i + 3, k), False)
                    scatter(Block(2 * i + 2 + k, i + 1, k), False)
                    gate_col(Block(2 * i + 4 + k, i + 2, k), False)
            for b in (NE - 2, NE - 1):
                scatter(blk(b), False)
            more = pool.value_load(n_ovf[0:1, 0:1], min_val=0, max_val=NOVF)
            with pool.Fori(0, NOVF // 2) as i:
                with pool.If(2 * i < more):
                    for b, _ in pair_plan(i):
                        gate_col(b, False)
                        gather(Block(b.n + 2, b.half + 1, b.par), False)
                        scatter(b, False)
                    pool.wait_ge(S["tabs_set"], 1)
                    pool.wait_ge(scat[0], 16 * (NE // 2 + 1 + i))
                    pool.wait_ge(scat[1], 16 * (NE // 2 + 1 + i))
                    pool.memset(marks[:, 0:1], 0.0)
                pool.nop()
            pool.wait_ge(scat[0], 16 * (NE // 2))
            pool.wait_ge(scat[1], 16 * (NE // 2))
            pool.wait_ge(gath[0], 16 * (NE // 2 + 1))
            pool.wait_ge(gath[1], 16 * (NE // 2 + 1))
            pool.memset(marks[:, 0:1], 0.0).then_inc(S["moe_done_p"], 1)

        @block.tensor
        def _(pe):
            def three(out_ap, a, b, first, last):
                pe.matmul(out_ap, a[0], b[0], start=first, stop=False)
                pe.matmul(out_ap, a[0], b[1], start=False, stop=False)
                return pe.matmul(out_ap, a[1], b[0], start=False, stop=last)

            pe.wait_ge(S["consts_set"], 1)
            pe.wait_ge(S["params_in"], 160)
            pe.transpose(b7[:, 0:NROWS], prm[0:NROWS, :], ident[0:NROWS, 0:NROWS]).then_inc(S["params_turned"], 1)
            pe.wait_ge(S["silu_set"], 1)
            for n in range(N_ADA1):
                piece_wait(pe, n)
                for h in range(PIECE // P):
                    at = 2 * (2 * n + h)
                    for j in range(KT):
                        mm = pe.matmul(b6[:, at:at + 2], piece[n % RING][:, j, P * h:P * h + P],
                                       silu_c[:, j:2 * KT:KT], start=(j == 0), stop=(j == KT - 1))
                mm.then_inc(S["ada1_used"], 1)
            for u, (g, j) in enumerate(units):
                t0, nt, _ = groups[g]
                if j == 0:
                    pe.wait_ge(S["xs_set"], t0 + nt)
                if u >= 4:
                    pe.wait_ge(S["unit_h"], u - 3)
                for t in range(nt):
                    mm = pe.transpose(bank(u)[:, P * t:P * t + P], x_all[:, t0 + t, P * j:P * j + P], ident[:])
                mm.then_inc(S["turned"], 1)

            def main_tile(n, slot, turn, with_ctx):
                pe.wait_ge(S["m_lo"], n + 1)
                if turn is not None:
                    pe.wait_ge(free[slot], turn)
                w = (ws_hi[slot], ws_lo[slot])
                for j in range(KT):
                    for h in range(2):
                        mm = three(main[:, slot, 512 * h:512 * h + 512], (w[0][:, j, :], w[1][:, j, :]),
                                   (h_hi[:, j, 512 * h:512 * h + 512], h_lo[:, j, 512 * h:512 * h + 512]),
                                   j == 0, j == KT - 1)
                if with_ctx is not None:
                    if with_ctx:
                        pe.wait_ge(S["ctx_free"], with_ctx)
                    for j in range(KT):
                        mm = three(b6[:, 0:CTX], (w[0][:, j, :], w[1][:, j, :]), (hc_hi[:, j, :], hc_lo[:, j, :]),
                                   j == 0, j == KT - 1)
                mm.then_inc(S["main_done"], 1)

            count = {"g": 0}

            def gates_of(c, d):
                pe.wait_ge(S["xc_set"], c + 1)
                if c == 0 and d == 0:
                    pe.wait_ge(S["gate_w_in"], 8 * 16)
                for kind in range(2):
                    w = gate_w[:, c, 2 * d + kind, :]
                    for part in range(3):
                        g = count["g"]
                        if g >= 3:
                            pe.wait_ge(S["gate_free"], g - 2)
                        if part < 2:
                            mm = pe.matmul(lat[:, part, :], w, xc[:, LAT + 512 * part:LAT + 512 * part + 512], start=True, stop=True)
                        else:
                            mm = pe.matmul(b7[:, 0:CTX], w, xc[:, 0:CTX], start=True, stop=True)
                        mm.then_inc(S["gate_done"], 1)
                        count["g"] += 1

            pe.wait_ge(S["unit_lo"], len(units))
            xr_seen = 0
            after_tile = {2: (0, 0), 3: (0, 1), 4: (1, 0), 5: (1, 1), 6: (2, 0), 7: (2, 1), 8: (3, 0)}
            for n in range(10):
                is_xr = what[n][0] == "xr"
                main_tile(n, n % 2, n // 2 if n >= 2 else None, xr_seen if is_xr else None)
                xr_seen += is_xr
                if n in after_tile:
                    gates_of(*after_tile[n])
            gates_of(3, 1)

            def row_cast(a):
                pe.wait_ge(S["acc_set"], a + 1)
                if a >= 2:
                    pe.wait_ge(S["row_set"], a - 1)
                if a == 0:
                    pe.wait_ge(S["adab2_in"], 16)
                    pe.wait_ge(S["ctx_free"], CT)
                w, at = divmod(a * PIECE, D)
                o = (b7, b6)[a % 2][:, 0:PIECE]
                pe.matmul(o, ones[:], rows[:, w, at:at + PIECE], start=True, stop=False)
                pe.matmul(o, ident[0:16, a:a + 1].to_broadcast([16, P]), adab2[:], start=False, stop=True)\
                    .then_inc(S["bc_done"], 1)

            for n in range(10, N_MAIN):
                main_tile(n, n % 2, n // 2, None)
                for k in range(2):
                    if n >= 12:
                        row_cast(2 * (n - 12) + k)

            def turn_m(t):
                pe.wait_ge(S["m_set"], t + 1)
                if t:
                    pe.wait_ge(S["mT_set"], t)
                for j in range(KT):
                    mm = pe.transpose(lat[:, j // 4, P * (j % 4):P * (j % 4) + P], m_row[t % 2][:, P * j:P * j + P], ident[:])
                mm.then_inc(S["mturn_done"], 1)

            def logits(t):
                pe.wait_ge(S["mT_set"], t + 1)
                if t == 0:
                    pe.wait_ge(S["route_in"], 64)
                o = b6[:, (NG + NE) * t:(NG + NE) * (t + 1)]
                for j in range(KT):
                    pe.matmul(o, mT[t % 2][:, j, :], w_route[:, j, :], start=(j == 0), stop=False)
                pe.matmul(o, ones[0:1, :], b_route[:], start=False, stop=True).then_inc(S["logit_done"], 1)

            for t in range(NT):
                slot = t % 2
                pe.wait_ge(free[slot], (N_MAIN + t) // 2)
                if t == 0:
                    pe.wait_ge(S["ylo_set"], KT)
                for j in range(KT):
                    if t == 0 and j % 2 == 0:
                        pe.wait_ge(S["wo_lo_s"], j // 2 + 1)
                    for h in range(2):
                        mm = three(main[:, slot, 512 * h:512 * h + 512],
                                   (y_hi[j][:, P * t:P * t + P], y_lo[j][:, P * t:P * t + P]),
                                   (wo_hi[:, j, 512 * h:512 * h + 512], wo_lo[:, j, 512 * h:512 * h + 512]),
                                   j == 0, j == KT - 1)
                mm.then_inc(S["main_done"], 1)
                if t >= 1:
                    turn_m(t - 1)
                if t >= 2:
                    logits(t - 2)
            turn_m(NT - 1)
            logits(NT - 2)
            logits(NT - 1)

            pe.wait_ge(S["hot_set"], 1)
            pe.matmul(b7[:, 0:NT * NE], tri[:], hot_s[:].rearrange("p t e -> p (t e)"), start=True, stop=False)
            pe.matmul(b7[:, 0:NT * NE], ones[:], pre[:, 0:NT, :].rearrange("p t e -> p (t e)"), start=False, stop=True)
            pe.matmul(b6[:, 0:NE], ones[:], pre[:, NT, :], start=True, stop=True).then_inc(S["cum_done"], 1)
            pe.wait_ge(S["tabs_in"], 1)
            for n in range(TOPK * NT):
                mm = pe.matmul(b7[:, 0:2 * NB], slot_hot[:, n, :], blk_hot[:, n, :, :].rearrange("p a b -> p (a b)"),
                               start=(n == 0), stop=(n == TOPK * NT - 1))
            mm.then_inc(S["tabs_done"], 1)

            def turn_x(b, first):
                pe.wait_ge(gath[b.par], 16 * b.half + 16)
                if not first:
                    pe.wait_ge(S["xl_set"], b.n)
                for j in range(KT):
                    mm = pe.transpose(main[:, 0, P * j:P * j + P], x_e[b.par][:, j:D:KT], ident[:])
                mm.then_inc(S["tx_done"], 1)

            def product(c, stationary, outs, kt):
                per = kt // 2
                for hf in range(2):
                    k = (2 * c.slot + hf) % SPLIT
                    pe.wait_ge(S["lo_done"], 2 * c.n + hf + 1)
                    for jj in range(per):
                        j = hf * per + jj
                        for n, o in enumerate(outs):
                            at = 512 * (len(outs) * jj + n)
                            mm = three(o, (stationary[0][:, j, :], stationary[1][:, j, :]),
                                       (w_hi[k][:, at:at + 512], w_lo[k][:, at:at + 512]), j == 0, j == kt - 1)
                    mm.then_inc(S["unit_used"], 1)

            def gate_up(which, b, c, first):
                if which == "g":
                    pe.wait_ge(S["xl_set"], b.n + 1)
                if not first:
                    pe.wait_ge(S["silu_e" if which == "g" else "h_set"], b.n)
                product(c, (xT_hi, xT_lo), [lat[:, 0 if which == "g" else 1, :]], KT)
                

            def turn_h(b, first):
                pe.wait_ge(S["h_set"], b.n + 1)
                if not first:
                    pe.wait_ge(S["hl_set"], b.n)
                for j in range(FT):
                    mm = pe.transpose(b6[:, P * j:P * j + P], h_act[:, j:FF:FT], ident[:])
                mm.then_inc(S["th_done"], 1)

            def down(b, c, first):
                pe.wait_ge(S["hl_set"], b.n + 1)
                if not first:
                    pe.wait_ge(S["y_out"], b.n)
                product(c, (hT_hi, hT_lo), [main[:, 1, 0:512], main[:, 1, 512:1024]], FT)

            def step(b, cs, turn_next=True):
                gate_up("g", b, cs[0], False)
                turn_h(before(b), isinstance(b.n, int) and b.n == 1)
                gate_up("u", b, cs[1], False)
                if turn_next:
                    turn_x(after(b), False)
                down(before(b), cs[2], isinstance(b.n, int) and b.n == 1)

            b, cs = plain(0)
            turn_x(b, True)
            gate_up("g", b, cs[0], True)
            gate_up("u", b, cs[1], True)
            turn_x(after(b), False)
            step(*plain(1))
            step(*plain(2))
            with pe.Fori(0, LOOPS) as i:
                for k in range(2):
                    step(*step_plan(i, k))
            b, cs = plain(NE - 1)
            step(b, cs, False)
            turn_h(b, False)
            down(b, LAST, False)
            more = pe.value_load(n_ovf[0:1, 0:1], min_val=0, max_val=NOVF)
            with pe.Fori(0, NOVF // 2) as i:
                with pe.If(2 * i < more):
                    for b, cs in pair_plan(i):
                        turn_x(b, False)
                        gate_up("g", b, cs[0], False)
                        gate_up("u", b, cs[1], False)
                        turn_h(b, False)
                        down(b, cs[2], False)
                pe.nop()

        @block.scalar
        def _(act):
            own = Own(act, S["act_own"])
            act.wait_ge(S["params_set"], 1)
            act.activation(silu_c[:], cols("c"), ACT.Silu).then_inc(S["silu_set"], 1)
            act.wait_ge(S["lam_w"], 1)
            act.activation(spt[:, 1, :], spt[:, 0, :], ACT.Exp, scale=-1.0).then_inc(S["lam_exp"], 1)
            act.wait_ge(S["lam_w"], 2)
            act.activation(spt[:, 3, :], spt[:, 2, :], ACT.Ln).then_inc(S["lam_ln"], 1)

            def squares(g):
                t0, nt, _ = groups[g]
                act.wait_ge(S[("x0_in", "x1_in", "xc_in")[g]], 16)
                for t in range(t0, t0 + nt):
                    own.wait()
                    own.did(act.activation(lat[:].rearrange("p a n -> p (a n)"), x_all[:, t, :], ACT.Square,
                                           accum_out=ssq[:, t:t + 1]))
                own.wait()
                act.activation(std[:, t0:t0 + nt], ssq[:, t0:t0 + nt], ACT.Sqrt, scale=1.0 / D, bias=eps[:])\
                    .then_inc(S["std_set"], 1)

            def unit(u):
                g, j = units[u]
                t0, nt, is_ctx = groups[g]
                n = P * nt
                dst = hc_hi[:, j, :] if is_ctx else h_hi[:, j, P * t0:P * t0 + n]
                act.wait_ge(S["unit_h"], u + 1)
                act.activation(dst, h_tmp[:, u % 2, 0:n], ACT.Copy).then_inc(S["unit_hi"], 1)

            def split(n):
                pn = piece_no[("w", n // 2)]
                piece_wait(act, pn)
                if n >= 2:
                    act.wait_ge(S["main_done"], n - 1)
                src = piece[pn % RING][:, :, P * (n % 2):P * (n % 2) + P]
                act.activation(ws_hi[n % 2][:], src, ACT.Copy).then_inc(S["m_hi"], 1)

            act.wait_ge(S["coef_set"], 1)
            squares(0)
            for u in range(8):
                unit(u)
            split(0)
            squares(1)
            for u in range(8, 16):
                unit(u)
            squares(2)
            for u in range(16, 24):
                unit(u)
            split(1)

            count = {"g": 0, "y": 0}

            def ri(c, d):
                for kind in range(2):
                    dst = (r_a, i_h[d])[kind]
                    k = 2 * c + d
                    if kind == 0 and k >= 1:
                        act.wait_ge(S["scan_done"], k)
                    if kind == 1 and c >= 1:
                        act.wait_ge(S["ylo_set" if d == 0 else "y_set"], c)
                    for part in range(3):
                        g = count["g"]
                        act.wait_ge(S["gate_done"], g + 1)
                        src = lat[:, part, :] if part < 2 else b7[:, 0:CTX]
                        to = dst[:, LAT + 512 * part:LAT + 512 * part + 512] if part < 2 else dst[:, 0:CTX]
                        act.activation(to, src, ACT.Sigmoid, bias=col(("ba", "bx")[kind], CT * d + c))\
                            .then_inc(S["gate_free"], 1)
                        count["g"] += 1
                act.wait_ge(S["gate_free"], count["g"])
                if k >= 1:
                    act.wait_ge(S["s2_set"], k)
                act.activation(t_s[:], r_a[:], ACT.Tanh, scale=q8[:, CT * d + c:CT * d + c + 1]).then_inc(S["tanh_set"], 1)
                act.wait_ge(S["tanh_set"], k + 1)
                act.activation(r_a[:], r_a[:], ACT.Exp, scale=nq8[:, CT * d + c:CT * d + c + 1]).then_inc(S["exp_set"], 1)

            def root(c, d):
                act.wait_ge(S["s2_set"], 2 * c + d + 1)
                act.activation(v_s[:], v_s[:], ACT.Sqrt).then_inc(S["s_set"], 1)

            def post(n):
                kind, c = what[n]
                act.wait_ge(S["main_done"], n + 1)
                src = main[:, n % 2, :]
                if kind == "xr":
                    act.wait_ge(S["pads_set"], 6)
                    if c:
                        act.wait_ge(S["xc_set"], c)
                    act.activation(xr_pad[:, 2:2 + CTX], b6[:, 0:CTX], ACT.Copy).then_inc(S["ctx_free"], 1)
                    act.activation(xr_pad[:, LAT + 2:LAT + 2 + SEQ], src, ACT.Copy).then_inc(free[n % 2], 1)
                elif kind == "gr":
                    if c >= 2:
                        act.wait_ge(S["y_set"], c - 1)
                    act.activation(gelu_g[c % 2][:], src, ACT.Gelu_apprx_tanh).then_inc(free[n % 2], 1)
                elif kind == "cg":
                    if c == 1:
                        act.wait_ge(S["ylo_set"], CT)
                    elif c >= 2:
                        act.wait_ge(S["u_set"], 3 * (c - 1))
                    act.activation(conv_u[c % 2][:], src, ACT.Copy).then_inc(free[n % 2], 1)

            def y_high(tile):
                act.wait_ge(S["y_set"], tile + 1)
                src = i_h[0][:, LAT:XC] if tile < CT else conv_y[tile % 2][:]
                if tile >= CT:
                    act.wait_ge(S["ylo_set"], CT)
                act.activation(y_hi[tile][:], src, ACT.Copy).then_inc(S["yhi_set"], 1)

            run = {"split": split, "post": post, "ri": ri, "root": root, "yhi": y_high}
            for name, *at in ACT_ORDER:
                run[name](*at)

            for i in range(4):
                pn = piece_no[("wo", i)]
                piece_wait(act, pn)
                if i == 0:
                    act.wait_ge(S["main_done"], N_MAIN)
                act.activation(wo_hi[:, 2 * i:2 * i + 2, :].rearrange("p j n -> p (j n)"),
                               piece[pn % RING][:].rearrange("p j n -> p (j n)"), ACT.Copy).then_inc(S["wo_hi_s"], 1)

            def mT_copy(t):
                act.wait_ge(S["mturn_done"], t + 1)
                if t >= 2:
                    act.wait_ge(S["logit_done"], t - 1)
                act.activation(mT[t % 2][:].rearrange("p j n -> p (j n)"), lat[:].rearrange("p a n -> p (a n)"), ACT.Copy)\
                    .then_inc(S["mT_set"], 1)

            for t in range(NT):
                act.wait_ge(S["x1_set"], t + 1)
                if t >= 2:
                    act.wait_ge((S["m_out0"], S["m_out1"])[t % 2], 16 * (t // 2))
                    act.wait_ge(S["mturn_done"], t - 1)
                act.activation(m_row[t % 2][:], x1[t % 2][:], ACT.Square, accum_out=ssq[:, t:t + 1]).then_inc(S["act_own"], 1)
                own.n += 1
                own.wait()
                act.activation(std[:, t:t + 1], ssq[:, t:t + 1], ACT.Sqrt, scale=1.0 / D, bias=eps[:]).then_inc(S["std_set"], 1)
                if t:
                    mT_copy(t - 1)
            mT_copy(NT - 1)
            act.wait_ge(S["logit_done"], NT)
            act.activation(logit[:].rearrange("p t n -> p (t n)"), b6[:, 0:NT * (NG + NE)], ACT.Copy).then_inc(S["logit_set"], 1)
            act.wait_ge(S["rexp_in"], 1)
            act.activation(xe[:], xs[:], ACT.Exp).then_inc(S["rexp_set"], 1)

            def hi(c, hf):
                k = (2 * c.slot + hf) % SPLIT
                act.wait_ge(raw_in[c.slot], 16 * c.turn + 16)
                if not (isinstance(c.n, int) and c.n < SPLIT // 2):
                    act.wait_ge(S["unit_used"], 2 * c.n + hf + 1 - SPLIT)
                act.activation(w_hi[k][:], raw[c.slot][:, UNIT * hf:UNIT * hf + UNIT], ACT.Copy).then_inc(S["hi_done"], 1)

            def x_high(b, first):
                act.wait_ge(S["tx_done"], b.n + 1)
                if not first:
                    act.wait_ge(S["unit_used"], up_units(b))
                act.activation(xT_hi[:].rearrange("p j n -> p (j n)"), main[:, 0, :], ACT.Copy).then_inc(S["xh_set"], 1)

            def silu(b, c_gate, first):
                act.wait_ge(S["unit_used"], 2 * c_gate.n + 2)
                if not first:
                    act.wait_ge(S["h_set"], b.n)
                act.activation(s_act[:], lat[:, 0, :], ACT.Silu).then_inc(S["silu_e"], 1)

            def h_high(b, c_prev_down):
                act.wait_ge(S["th_done"], b.n + 1)
                if c_prev_down is not None:
                    act.wait_ge(S["unit_used"], 2 * c_prev_down + 2)
                act.activation(hT_hi[:].rearrange("p j n -> p (j n)"), b6[:], ACT.Copy).then_inc(S["hh_set"], 1)

            def y_out(b, c_down):
                act.wait_ge(S["unit_used"], 2 * c_down + 2)
                act.wait_ge(S["ex_gate"], b.n + 1)
                if not (isinstance(b.n, int) and b.n < 2):
                    act.wait_ge(scat[b.par], 16 * b.half)
                act.activation(y_e[b.par][:], main[:, 1, :], ACT.Copy, scale=gate_now[b.par][:]).then_inc(S["y_out"], 1)

            def up_units(b):
                return 2 * (3 * (b.n - 1)) + 2 if not (isinstance(b.n, int) and b.n == 1) else 4

            def step(b, cs, last=False):
                n = b.n if isinstance(b.n, int) else 99
                hi(cs[1], 0)
                if n >= 2:
                    y_out(before(before(b)), cs[0].n - 1)
                hi(cs[1], 1)
                silu(b, cs[0], n == 0)
                if n >= 1:
                    h_high(before(b), cs[0].n - 1 if n >= 2 else None)
                    hi(cs[2], 0)
                    hi(cs[2], 1)
                if not last:
                    x_high(after(b), False)
                    nxt = Chunk(cs[2].n + 1, (cs[2].slot + 1) % RAW, cs[2].turn + (cs[2].slot + 1) // RAW) if n >= 1 else plain(1)[1][0]
                    hi(nxt, 0)
                    hi(nxt, 1)

            b, cs = plain(0)
            x_high(b, True)
            hi(cs[0], 0)
            hi(cs[0], 1)
            step(b, cs)
            step(*plain(1))
            step(*plain(2))
            with act.Fori(0, LOOPS) as i:
                for k in range(2):
                    step(*step_plan(i, k))
            b, cs = plain(NE - 1)
            step(b, cs, True)
            h_high(b, cs[2].n)
            hi(LAST, 0)
            hi(LAST, 1)
            y_out(before(b), cs[2].n)
            y_out(b, LAST.n)
            more = act.value_load(n_ovf[0:1, 0:1], min_val=0, max_val=NOVF)
            with act.Fori(0, NOVF // 2) as i:
                with act.If(2 * i < more):
                    for b, cs in pair_plan(i):
                        act.wait_ge(S["tx_done"], b.n + 1)
                        act.activation(xT_hi[:].rearrange("p j n -> p (j n)"), main[:, 0, :], ACT.Copy).then_inc(S["xh_set"], 1)
                        for c in cs[0:2]:
                            hi(c, 0)
                            hi(c, 1)
                        silu(b, cs[0], False)
                        h_high(b, None)
                        hi(cs[2], 0)
                        hi(cs[2], 1)
                        y_out(b, cs[2].n)
                act.nop()
            act.activation(std[:, 15:16], ssq[:, 0:1], ACT.Copy).then_inc(S["moe_done_a"], 1)
            for t in range(NT):
                act.wait_ge(S["fsum"], t + 1)
                act.activation(fin[t % 4][:, 3, :], fin[t % 4][:, 2, :], ACT.Square, accum_out=ssq[:, t:t + 1]).then_inc(S["fsq"], 1)
                act.wait_ge(S["fsq"], t + 1)
                act.activation(std[:, t:t + 1], ssq[:, t:t + 1], ACT.Sqrt, scale=1.0 / D, bias=eps[:]).then_inc(S["fstd"], 1)

        @block.vector
        def _(dve):
            own = Own(dve, S["dve_own"])

            def tt(o, a, b, op):
                own.did(dve.tensor_tensor(o, a, b, op))

            def ts(o, a, s1, s2, op0, op1=None):
                own.did(dve.tensor_scalar(o, a, s1, s2, op0, op1) if op1 is not None else dve.tensor_scalar(o, a, s1, None, op0))

            own.did(dve.memset(eps[:], EPS))
            dve.wait_ge(S["params_turned"], 1)
            dve.tensor_copy(prmT[:], b7[:, 0:NROWS]).then_inc(S["params_set"], 1)
            dve.wait_ge(S["params_set"], 1)
            lam = cols("lam")
            own.did(dve.tensor_scalar(spt[:, 4, :], lam, -1.0, None, ALU.mult))
            own.wait()
            dve.tensor_tensor(spt[:, 0, :], lam, spt[:, 4, :], ALU.max).then_inc(S["lam_w"], 1)
            dve.wait_ge(S["lam_exp"], 1)
            dve.tensor_scalar(spt[:, 2, :], spt[:, 1, :], 1.0, None, ALU.add).then_inc(S["lam_w"], 1)
            dve.wait_ge(S["lam_w"], 2)
            ts(spt[:, 0, :], spt[:, 2, :], -1.0, None, ALU.add)
            dve.wait_ge(S["lam_ln"], 1)
            own.wait()
            ts(spt[:, 2, :], spt[:, 0, :], 0.0, None, ALU.is_equal)
            own.wait()
            tt(spt[:, 0, :], spt[:, 0, :], spt[:, 2, :], ALU.add)
            tt(spt[:, 3, :], spt[:, 3, :], spt[:, 2, :], ALU.add)
            own.wait()
            own.did(dve.reciprocal(spt[:, 0, :], spt[:, 0, :]))
            tt(spt[:, 3, :], spt[:, 3, :], spt[:, 1, :], ALU.mult)
            own.wait()
            tt(spt[:, 3, :], spt[:, 3, :], spt[:, 0, :], ALU.mult)
            ts(spt[:, 4, :], spt[:, 4, :], 0.0, None, ALU.max)
            own.wait()
            tt(spt[:, 3, :], spt[:, 3, :], spt[:, 4, :], ALU.add)
            own.wait()
            ts(q8[:], spt[:, 3, :], RG_C, None, ALU.mult)
            dve.tensor_scalar(nq8[:], spt[:, 3, :], -RG_C, None, ALU.mult).then_inc(S["coef_set"], 1)

            def scale_rows(g):
                t0, nt, _ = groups[g]
                dve.wait_ge(S["std_set"], g + 1)
                own.did(dve.reciprocal(rstd[:, t0:t0 + nt], std[:, t0:t0 + nt]))
                own.wait()
                for t in range(t0, t0 + nt):
                    dve.tensor_scalar(x_all[:, t, :], x_all[:, t, :], rstd[:, t:t + 1], None, ALU.mult).then_inc(S["xs_set"], 1)

            scale_rows(0)
            dve.wait_ge(S["ada1_used"], N_ADA1)
            mod = b6[:, 0:4 * KT].rearrange("p (w j s) -> p w s j", w=2, s=2)
            ab = cols("ada_b").rearrange("p (w j) -> p w j", w=2)
            for s in range(2):
                tt(mod_s[:, s, :], mod[:, 0, s, :], ab[:, 0, :], ALU.add)
                own.did(dve.scalar_tensor_tensor(out=mod_a[:, s, :], in0=mod[:, 1, s, :], scalar=1.0, in1=ab[:, 1, :],
                                                 op0=ALU.add, op1=ALU.add))
                own.wait()
                tt(mod_a[:, s, :], mod_a[:, s, :], cols("g1n"), ALU.mult)
            own.wait()

            def unit_h(u):
                g, j = units[u]
                t0, nt, s = groups[g]
                dve.wait_ge(S["turned"], u + 1)
                if u >= 2:
                    dve.wait_ge(S["unit_lo"], u - 1)
                dve.tensor_scalar(h_tmp[:, u % 2, 0:P * nt], bank(u)[:, 0:P * nt], mod_a[:, s, j:j + 1], mod_s[:, s, j:j + 1],
                                  ALU.mult, ALU.add).then_inc(S["unit_h"], 1)

            def unit_l(u):
                g, j = units[u]
                t0, nt, is_ctx = groups[g]
                n = P * nt
                hi_, lo_ = ((hc_hi[:, j, :], hc_lo[:, j, :]) if is_ctx else
                            (h_hi[:, j, P * t0:P * t0 + n], h_lo[:, j, P * t0:P * t0 + n]))
                dve.wait_ge(S["unit_hi"], u + 1)
                dve.tensor_tensor(lo_, h_tmp[:, u % 2, 0:n], hi_, ALU.subtract).then_inc(S["unit_lo"], 1)

            def unit_run(a, b):
                for u in range(a, b):
                    unit_h(u)
                    if u > a:
                        unit_l(u - 1)
                unit_l(b - 1)

            used = {"n": 0}

            def split(n):
                pn = piece_no[("w", n // 2)]
                dve.wait_ge(S["m_hi"], n + 1)
                src = piece[pn % RING][:, :, P * (n % 2):P * (n % 2) + P]
                dve.tensor_tensor(ws_lo[n % 2][:], src, ws_hi[n % 2][:], ALU.subtract).then_inc(S["m_lo"], 1)
                if n % 2:
                    release(pn)

            def release(pn):
                assert pn == N_ADA1 + used["n"], (pn, used)
                used["n"] += 1
                last = kinds[pn]
                if last[0] == "w":
                    dve.wait_ge(S["m_lo"], 2 * last[1] + 2)
                else:
                    own.wait()
                dve.memset(marks[:, 1:2], 0.0).then_inc(S["piece_used"], 1)
                dve.wait_ge(S["piece_used"], used["n"])

            unit_run(0, 8)
            split(0)
            scale_rows(1)
            unit_run(8, 16)
            scale_rows(2)
            unit_run(16, 24)
            split(1)

            def conv(c):
                dve.wait_ge(free[what_index[("xr", c)] % 2], what_index[("xr", c)] // 2 + 1)
                if c:
                    dve.wait_ge(S["gate_done"], 12 * c)
                    own.wait()
                own.did(dve.tensor_scalar(xc[:], xr_pad[:, 0:XC], col("conv_w", c), col("conv_b", c), ALU.mult, ALU.add))
                for k in range(1, TAPS):
                    own.wait()
                    ins = dve.scalar_tensor_tensor(out=xc[:], in0=xr_pad[:, k:k + XC], scalar=col("conv_w", CT * k + c),
                                                   in1=xc[:], op0=ALU.mult, op1=ALU.add)
                    if k < TAPS - 1:
                        own.did(ins)
                    else:
                        ins.then_inc(S["xc_set"], 1)

            def scan(c, d):
                k = 2 * c + d
                dve.wait_ge(S["exp_set"], k + 1)
                own.wait()
                tt(v_s[:], r_a[:], r_a[:], ALU.mult)
                own.wait()
                dve.scalar_tensor_tensor(out=v_s[:], in0=v_s[:], scalar=1.0, in1=t_s[:], op0=ALU.add, op1=ALU.mult)\
                    .then_inc(S["s2_set"], 1)
                dve.wait_ge(S["xc_set"], c + 1)
                tt(i_h[d][:], i_h[d][:], xc[:], ALU.mult)
                dve.wait_ge(S["s_set"], k + 1)
                own.wait()
                tt(i_h[d][:], i_h[d][:], v_s[:], ALU.mult)
                own.wait()
                b = i_h[d]
                if d == 0:
                    own.did(dve.tensor_tensor_scan(b[:, 0:CTX], r_a[:, 0:CTX], b[:, 0:CTX], 0.0, ALU.mult, ALU.add))
                    own.wait()
                    dve.tensor_tensor_scan(b[:, LAT:XC], r_a[:, LAT:XC], b[:, LAT:XC], b[:, CTX - 1:CTX], ALU.mult, ALU.add)\
                        .then_inc(S["scan_done"], 1)
                else:
                    own.did(dve.tensor_tensor_scan(b[:, CTX - 1::-1], r_a[:, CTX - 1::-1], b[:, CTX - 1::-1], 0.0, ALU.mult, ALU.add))
                    own.wait()
                    dve.tensor_tensor_scan(b[:, XC - 1:CTX + 2:-1], r_a[:, XC - 1:CTX + 2:-1], b[:, XC - 1:CTX + 2:-1], b[:, 0:1],
                                           ALU.mult, ALU.add).then_inc(S["scan_done"], 1)

            def y_rnn(c):
                dve.wait_ge(S["scan_done"], 2 * c + 2)
                n = what_index[("gr", c)]
                dve.wait_ge(free[n % 2], n // 2 + 1)
                y = i_h[0][:, LAT:XC]
                tt(y, y, i_h[1][:, LAT:XC], ALU.add)
                own.wait()
                dve.tensor_tensor(y, y, gelu_g[c % 2][:], ALU.mult).then_inc(S["y_set"], 1)

            def y_low(tile):
                dve.wait_ge(S["yhi_set"], tile + 1)
                src = i_h[0][:, LAT:XC] if tile < CT else conv_y[tile % 2][:]
                dve.tensor_tensor(y_lo[tile][:], src, y_hi[tile][:], ALU.subtract).then_inc(S["ylo_set"], 1)
                dve.wait_ge(S["ylo_set"], tile + 1)

            def conv_v(n):
                _, c = what[n]
                cg = what_index[("cg", c)]
                dve.wait_ge(S["main_done"], n + 1)
                dve.wait_ge(free[cg % 2], cg // 2 + 1)
                u, y = conv_u[c % 2], conv_y[c % 2]
                dve.tensor_tensor(u[:], main[:, n % 2, :], u[:], ALU.mult).then_inc(free[n % 2], 1)
                dve.wait_ge(free[n % 2], n // 2 + 1)
                dve.tensor_scalar(y[:], u[:], col("sc_w", CT + c), None, ALU.mult).then_inc(S["u_set"], 1)
                dve.wait_ge(S["u_set"], 3 * c + 1)
                if c < CT // 2:
                    ug, yg = (t[:].rearrange("p (r w) -> p r w", w=GRID_W) for t in (u, y))
                    sh = [(yg[:, :, 1:GRID_W], ug[:, :, 0:GRID_W - 1]), (yg[:, :, 0:GRID_W - 1], ug[:, :, 1:GRID_W])]
                else:
                    sh = [(y[:, GRID_W:SEQ], u[:, 0:SEQ - GRID_W]), (y[:, 0:SEQ - GRID_W], u[:, GRID_W:SEQ])]
                for k, (o, i) in enumerate(sh):
                    dve.scalar_tensor_tensor(out=o, in0=i, scalar=col("sc_w", 2 * k * CT + c), in1=o, op0=ALU.mult, op1=ALU.add)\
                        .then_inc(S["u_set"], 1)
                    dve.wait_ge(S["u_set"], 3 * c + 2 + k)

            def conv_b(n):
                _, c = what[n]
                dve.wait_ge(S["main_done"], n + 1)
                y = conv_y[c % 2]
                dve.tensor_tensor(y[:], main[:, n % 2, :], y[:], ALU.mult).then_inc(free[n % 2], 1)
                dve.wait_ge(free[n % 2], n // 2 + 1)
                dve.memset(marks[:, 2:3], 0.0).then_inc(S["y_set"], 1)
                dve.wait_ge(S["y_set"], CT + c + 1)

            def ada2(a):
                pn = piece_no[("ada2", a)]
                piece_wait(dve, pn)
                if a == 0:
                    dve.wait_ge(S["main_done"], 6)
                w, at = divmod(a * PIECE, D)
                o = rows[:, w, at:at + PIECE]
                for j in range(KT):
                    src = piece[pn % RING][:, j, :]
                    if j == 0:
                        ins = dve.tensor_scalar(o, src, silu_c[:, j:j + 1], None, ALU.mult)
                    else:
                        ins = dve.scalar_tensor_tensor(out=o, in0=src, scalar=silu_c[:, j:j + 1], in1=o, op0=ALU.mult, op1=ALU.add)
                    if j < KT - 1:
                        own.did(ins)
                        own.wait()
                    else:
                        ins.then_inc(S["acc_set"], 1)
                dve.wait_ge(S["acc_set"], a + 1)
                release(pn)

            def row_out(a):
                dve.wait_ge(S["bc_done"], a + 1)
                w, at = divmod(a * PIECE, D)
                dve.tensor_copy(rows[:, w, at:at + PIECE], (b7, b6)[a % 2][:, 0:PIECE]).then_inc(S["row_set"], 1)

            run = {"split": split, "conv": conv, "scan": scan, "yrnn": y_rnn, "ylo": y_low, "v": conv_v, "b": conv_b,
                   "ada": ada2, "row": row_out}
            for name, *at in DVE_ORDER:
                run[name](*at)
            for i in range(4):
                pn = piece_no[("wo", i)]
                dve.wait_ge(S["wo_hi_s"], i + 1)
                own.did(dve.tensor_tensor(wo_lo[:, 2 * i:2 * i + 2, :].rearrange("p j n -> p (j n)"),
                                          piece[pn % RING][:].rearrange("p j n -> p (j n)"),
                                          wo_hi[:, 2 * i:2 * i + 2, :].rearrange("p j n -> p (j n)"), ALU.subtract))
                own.wait()
                dve.memset(marks[:, 3:4], 0.0).then_inc(S["wo_lo_s"], 1)
                dve.wait_ge(S["wo_lo_s"], i + 1)
                release(pn)

            dve.wait_ge(S["norm2_in"], 16)
            dve.wait_ge(S["row_set"], N_ADA2)
            own.did(dve.scalar_tensor_tensor(out=rows[:, 2, :], in0=rows[:, 2, :], scalar=1.0, in1=norm2[:], op0=ALU.add, op1=ALU.mult))
            own.wait()

            for t in range(NT):
                par = t % 2
                dve.wait_ge(S["main_done"], N_MAIN + t + 1)
                dve.wait_ge((S["x_in0"], S["x_in1"])[par], 16 * (t // 2) + 16)
                dve.wait_ge(S["row_set"], N_ADA2)
                if t >= 2:
                    dve.wait_ge((S["x1_out0"], S["x1_out1"])[par], 16 * (t // 2))
                dve.tensor_tensor(x1[par][:], main[:, par, :], rows[:, 0, :], ALU.mult).then_inc(free[par], 1)
                dve.wait_ge(free[par], (N_MAIN + t) // 2 + 1)
                dve.tensor_tensor(x1[par][:], x1[par][:], x_in[par][:], ALU.add).then_inc(S["x1_set"], 1)
                dve.wait_ge(S["std_set"], 3 + t + 1)
                own.did(dve.reciprocal(rstd[:, t:t + 1], std[:, t:t + 1]))
                own.wait()
                own.did(dve.scalar_tensor_tensor(out=m_row[par][:], in0=x1[par][:], scalar=rstd[:, t:t + 1], in1=rows[:, 2, :],
                                                 op0=ALU.mult, op1=ALU.mult))
                own.wait()
                dve.tensor_tensor(m_row[par][:], m_row[par][:], rows[:, 1, :], ALU.add).then_inc(S["m_set"], 1)

            def bc(ap, shape):
                return ap.to_broadcast(shape)

            dve.wait_ge(S["x1_out0"], 16 * (NT // 2))
            dve.wait_ge(S["x1_out1"], 16 * (NT // 2))
            dve.wait_ge(S["logit_set"], 1)
            own.did(dve.memset(g_pad[:], -3.0e38))
            own.did(dve.memset(pre[:, 0, :], 0.0))
            own.wait()
            own.did(dve.tensor_copy(g_pad[:, :, 0:NG], logit[:, :, 0:NG]))
            own.wait()
            for t in range(NT):
                own.did(dve.max(g_top[:, t, :], g_pad[:, t, :]))
            own.wait()
            for t in range(NT):
                own.did(dve.max_index(g_idx[:, t, :], g_top[:, t, :], g_pad[:, t, :]))
            own.wait()
            own.did(dve.tensor_copy(gi[:], g_idx[:, :, 0]))
            tt(xs[:, :, 0:NG], logit[:, :, 0:NG], bc(g_top[:, :, 0:1], [P, NT, NG]), ALU.subtract)
            own.wait()
            tt(g_hot[:], iota[:, 0:NG].unsqueeze(1).to_broadcast([P, NT, NG]), gi[:].unsqueeze(2).to_broadcast([P, NT, NG]), ALU.is_equal)
            own.wait()
            for g in range(NG):
                src = logit[:, :, NG + EPG * g:NG + EPG * g + EPG]
                hot_g = bc(g_hot[:, :, g:g + 1], [P, NT, EPG])
                if g == 0:
                    tt(e8[:], src, hot_g, ALU.mult)
                else:
                    tt(big[:, :, 0:EPG], src, hot_g, ALU.mult)
                    own.wait()
                    tt(e8[:], e8[:], big[:, :, 0:EPG], ALU.add)
                own.wait()
            for t in range(NT):
                own.did(dve.max(e_top[:, t, :], e8[:, t, :]))
            own.wait()
            for t in range(NT):
                own.did(dve.max_index(e_idx[:, t, :], e_top[:, t, :], e8[:, t, :]))
            tt(xs[:, :, NG:NG + EPG], e8[:], bc(e_top[:, :, 0:1], [P, NT, EPG]), ALU.subtract)
            own.wait()
            dve.tensor_tensor(xs[:, :, 12:14], e_top[:, :, 0:2], bc(e_top[:, :, 0:1], [P, NT, 2]), ALU.subtract).then_inc(S["rexp_in"], 1)
            for k in range(TOPK):
                own.did(dve.tensor_copy(e_k[:, k, :], e_idx[:, :, k]))
            own.wait()
            for k in range(TOPK):
                own.did(dve.scalar_tensor_tensor(out=e_k[:, k, :], in0=gi[:], scalar=float(EPG), in1=e_k[:, k, :],
                                                 op0=ALU.mult, op1=ALU.add))
            own.wait()
            for k in range(TOPK):
                tt(hot[:, k, :, :], iota[:, 0:NE].unsqueeze(1).to_broadcast([P, NT, NE]),
                   e_k[:, k, :].unsqueeze(2).to_broadcast([P, NT, NE]), ALU.is_equal)
            own.wait()
            tt(hot_s[:], hot[:, 0, :, :], hot[:, 1, :, :], ALU.add)
            for t in range(NT):
                own.wait()
                if t < NT - 1:
                    tt(pre[:, t + 1, :], pre[:, t, :], hot_s[:, t, :], ALU.add)
                else:
                    dve.tensor_tensor(pre[:, t + 1, :], pre[:, t, :], hot_s[:, t, :], ALU.add).then_inc(S["hot_set"], 1)
            dve.wait_ge(S["rexp_set"], 1)
            own.did(dve.tensor_reduce(dens[:, 0, :], xe[:, :, 0:NG], AX, ALU.add))
            own.did(dve.tensor_reduce(dens[:, 1, :], xe[:, :, NG:NG + EPG], AX, ALU.add))
            own.wait()
            own.did(dve.reciprocal(dens[:, 0:2, :], dens[:, 0:2, :]))
            own.wait()
            for k in range(TOPK):
                tt(gates[:, k, :], xe[:, :, 12 + k], dens[:, 1, :], ALU.mult)
            own.wait()
            tt(dens[:, 2, :], gates[:, 0, :], gates[:, 1, :], ALU.add)
            own.wait()
            own.did(dve.reciprocal(dens[:, 2, :], dens[:, 2, :]))
            own.wait()
            tt(dens[:, 3, :], dens[:, 0, :], dens[:, 2, :], ALU.mult)
            own.wait()
            for k in range(TOPK):
                tt(gates[:, k, :], gates[:, k, :], dens[:, 3, :], ALU.mult)
            dve.wait_ge(S["cum_done"], 1)
            for k in range(TOPK):
                own.wait()
                tt(big[:], hot[:, k, :, :], b7[:, 0:NT * NE].rearrange("p (t e) -> p t e", t=NT), ALU.mult)
                own.wait()
                own.did(dve.tensor_reduce(rank[:, k, :], big[:], AX, ALU.add))
            ts(cnt[:], b6[:, 0:NE], -1.0, 0.0, ALU.add, ALU.max)
            own.wait()
            own.did(dve.tensor_copy(cnt_i[:], cnt[:]))
            own.did(dve.tensor_copy(rank_i[:], rank[:]))
            own.wait()
            ts(cnt_i[:], cnt_i[:], 7, None, ALU.logical_shift_right)
            ts(bq_i[:], rank_i[:], 7, None, ALU.logical_shift_right)
            ts(s_i[:], rank_i[:], P - 1, None, ALU.bitwise_and)
            own.wait()
            own.did(dve.tensor_copy(extra[:], cnt_i[:]))
            own.did(dve.tensor_copy(bq[:], bq_i[:]))
            own.did(dve.tensor_copy(s_f[:], s_i[:]))
            own.wait()
            own.did(dve.tensor_tensor_scan(incl[:], ones_e[:], extra[:], 0.0, ALU.mult, ALU.add))
            own.wait()
            tt(excl[:], incl[:], extra[:], ALU.subtract)
            own.did(dve.tensor_copy(n_ovf[:], incl[:, NE - 1:NE]))
            tt(ovf_c[:], incl[:].unsqueeze(1).to_broadcast([P, NOVF, NE]), iota[:, 0:NOVF].unsqueeze(2).to_broadcast([P, NOVF, NE]), ALU.is_le)
            own.wait()
            own.did(dve.tensor_reduce(ov_f[:], ovf_c[:], AX, ALU.add))
            own.wait()
            ts(ov_f[:], ov_f[:], float(NE - 1), None, ALU.min)
            own.wait()
            own.did(dve.tensor_copy(ovf_exp[:], ov_f[:]))
            for k in range(TOPK):
                own.wait()
                tt(big[:], hot[:, k, :, :], excl[:].unsqueeze(1).to_broadcast([P, NT, NE]), ALU.mult)
                own.wait()
                own.did(dve.tensor_reduce(ov_k[:, k, :], big[:], AX, ALU.add))
            own.wait()
            tt(ov_k[:], ov_k[:], bq[:], ALU.add)
            own.wait()
            tt(ov_k[:], ov_k[:], e_k[:], ALU.subtract)
            ts(blk_k[:], bq[:], 1.0, None, ALU.min)
            own.wait()
            own.did(dve.scalar_tensor_tensor(out=ov_k[:], in0=ov_k[:], scalar=float(NE - 1), in1=blk_k[:], op0=ALU.add, op1=ALU.mult))
            own.wait()
            tt(blk_k[:], e_k[:], ov_k[:], ALU.add)
            own.wait()
            for k in range(TOPK):
                bh = blk_hot[:, NT * k:NT * k + NT, :, :]
                tt(bh[:, :, 0, :], iota[:, 0:NB].unsqueeze(1).to_broadcast([P, NT, NB]),
                   blk_k[:, k, :].unsqueeze(2).to_broadcast([P, NT, NB]), ALU.is_equal)
                for t in range(NT):
                    ts(slot_hot[:, NT * k + t, :], iota[:], s_f[:, k, t:t + 1], None, ALU.is_equal)
            own.wait()
            for k in range(TOPK):
                bh = blk_hot[:, NT * k:NT * k + NT, :, :]
                tt(bh[:, :, 1, :], bh[:, :, 0, :], gates[:, k, :].unsqueeze(2).to_broadcast([P, NT, NB]), ALU.mult)
            own.wait()
            for k in range(TOPK):
                bh = blk_hot[:, NT * k:NT * k + NT, :, :]
                ins = dve.tensor_tensor(bh[:, :, 0, :], bh[:, :, 0, :], tok_id[:, k, :].unsqueeze(2).to_broadcast([P, NT, NB]), ALU.mult)
                if k < TOPK - 1:
                    own.did(ins)
                    own.wait()
                else:
                    ins.then_inc(S["tabs_in"], 1)
            dve.wait_ge(S["tabs_done"], 1)
            own.did(dve.tensor_copy(slots_f[:].rearrange("p a b -> p (a b)"), b7[:, 0:2 * NB]))
            own.wait()
            own.did(dve.tensor_copy(gate_tab[:], slots_f[:, 1, :]))
            ts(slot_v[:], slots_f[:, 0, :], 0.0, float(NONE + 1), ALU.is_equal, ALU.mult)
            own.wait()
            own.did(dve.scalar_tensor_tensor(out=slot_v[:], in0=slots_f[:, 0, :], scalar=-1.0, in1=slot_v[:], op0=ALU.add, op1=ALU.add))
            own.wait()
            own.did(dve.tensor_copy(id_tab[:, 1:], slot_v[:]))
            own.wait()
            dve.tensor_scalar(tok_tab[:, 1:], id_tab[:, 1:], NONE + SEQ - 1, None, ALU.bitwise_and).then_inc(S["tabs_set"], 1)

            def lo(c, hf):
                k = (2 * c.slot + hf) % SPLIT
                dve.wait_ge(S["hi_done"], 2 * c.n + hf + 1)
                dve.tensor_tensor(w_lo[k][:], raw[c.slot][:, UNIT * hf:UNIT * hf + UNIT], w_hi[k][:], ALU.subtract)\
                    .then_inc(S["lo_done"], 1)

            def x_low(b):
                dve.wait_ge(S["xh_set"], b.n + 1)
                dve.tensor_tensor(xT_lo[:].rearrange("p j n -> p (j n)"), main[:, 0, :], xT_hi[:].rearrange("p j n -> p (j n)"),
                                  ALU.subtract).then_inc(S["xl_set"], 1)

            def h_mul(b, c_up, first):
                dve.wait_ge(S["silu_e"], b.n + 1)
                dve.wait_ge(S["unit_used"], 2 * c_up.n + 2)
                if not first:
                    dve.wait_ge(S["th_done"], b.n)
                dve.tensor_tensor(h_act[:], lat[:, 1, :], s_act[:], ALU.mult).then_inc(S["h_set"], 1)

            def h_low(b):
                dve.wait_ge(S["hh_set"], b.n + 1)
                dve.tensor_tensor(hT_lo[:].rearrange("p j n -> p (j n)"), b6[:], hT_hi[:].rearrange("p j n -> p (j n)"),
                                  ALU.subtract).then_inc(S["hl_set"], 1)

            def step(b, cs, last=False):
                n = b.n if isinstance(b.n, int) else 99
                lo(cs[1], 0)
                lo(cs[1], 1)
                if n >= 1:
                    h_low(before(b))
                    lo(cs[2], 0)
                    lo(cs[2], 1)
                h_mul(b, cs[1], n == 0)
                if not last:
                    x_low(after(b))
                    nxt = Chunk(cs[2].n + 1, (cs[2].slot + 1) % RAW, 0) if n >= 1 else plain(1)[1][0]
                    lo(nxt, 0)
                    lo(nxt, 1)

            b, cs = plain(0)
            x_low(b)
            lo(cs[0], 0)
            lo(cs[0], 1)
            step(b, cs)
            step(*plain(1))
            step(*plain(2))
            with dve.Fori(0, LOOPS) as i:
                for k in range(2):
                    step(*step_plan(i, k))
            b, cs = plain(NE - 1)
            step(b, cs, True)
            h_low(b)
            lo(LAST, 0)
            lo(LAST, 1)
            more = dve.value_load(n_ovf[0:1, 0:1], min_val=0, max_val=NOVF)
            with dve.Fori(0, NOVF // 2) as i:
                with dve.If(2 * i < more):
                    for b, cs in pair_plan(i):
                        x_low(b)
                        for c in cs[0:2]:
                            lo(c, 0)
                            lo(c, 1)
                        h_mul(b, cs[1], False)
                        h_low(b)
                        lo(cs[2], 0)
                        lo(cs[2], 1)
                dve.nop()
            dve.wait_ge(S["frow_in"], 32)
            for t in range(NT):
                f = fin[t % 4]
                dve.wait_ge(S[f"fx{t % 4}"], 32 * (t // 4) + 32)
                tt(f[:, 0, :], f[:, 0, :], f[:, 1, :], ALU.add)
                own.wait()
                tt(f[:, 0, :], f[:, 0, :], fin_rows[:, 0, :], ALU.mult)
                own.wait()
                if t >= 4:
                    dve.wait_ge(S[f"fo{t % 4}"], 16 * (t // 4))
                dve.tensor_tensor(f[:, 2, :], f[:, 2, :], f[:, 0, :], ALU.add).then_inc(S["fsum"], 1)
                dve.wait_ge(S["fstd"], t + 1)
                own.did(dve.reciprocal(rstd[:, t:t + 1], std[:, t:t + 1]))
                own.wait()
                dve.scalar_tensor_tensor(out=f[:, 3, :], in0=f[:, 2, :], scalar=rstd[:, t:t + 1], in1=fin_rows[:, 1, :],
                                         op0=ALU.mult, op1=ALU.mult).then_inc(S["fout"], 1)


_INS = ["x", "c", "ctx", "c_ctx", "ada_w", "ada_b", "norm1_g", "norm2_g", "w_in", "rnn_conv_w", "rnn_conv_b", "rg_wa",
        "rg_ba", "rg_wx", "rg_bx", "rg_lambda", "sc_conv_w", "w_out", "router_group_w", "router_group_b", "router_exp_w",
        "router_exp_b", "exp_w_gate", "exp_w_up", "exp_w_down", "final_norm_g"]


def kernel(**inputs):
    import concourse.bacc as bacc
    from concourse.bass_utils import run_bass_kernel_spmd

    nc = bacc.Bacc("TRN2", target_bir_lowering=False, num_devices=1)
    arrays, aps = {}, {}
    for name in _INS:
        a = np.ascontiguousarray(inputs[name])
        arrays[f"in_{name}"] = a
        aps[name] = nc.dram_tensor(f"in_{name}", a.shape, mybir.dt.from_np(a.dtype), kind="ExternalInput").ap()
    out = nc.dram_tensor("out_0", (1, SEQ, D), F32, kind="ExternalOutput").ap()
    layer(nc, aps, out)
    r = run_bass_kernel_spmd(nc, [arrays], core_ids=[0])
    return r.results[0]["out_0"]
```

```python
from contextlib import ExitStack

import numpy as np
import concourse.bass as bass
from concourse import mybir

F32 = mybir.dt.float32
F32R = mybir.dt.float32r
I32 = mybir.dt.int32
U32 = mybir.dt.uint32
ACT = mybir.ActivationFunctionType
ALU = mybir.AluOpType
AX = mybir.AxisListType.X

P = 128
D = 1024
KT = D // P
SEQ, CTX = 1024, 256
NT = SEQ // P
NTC = NT + CTX // P
GRID_W = 64
TAPS, CTAPS = 4, 3
CT = 512 // P
RG_C = 8.0
EPS = 1e-6
NG, EPG, NE = 4, 8, 32
FF = 512
FT = FF // P
TOPK = 2
NOVF = (TOPK * SEQ) // P
NB = NE + NOVF + 2
DVE_HOT = 4
POOL_G2 = (3, 5)
NONE = 4096
LAT = CTX + 3
XC = LAT + SEQ
XR = XC + TAPS - 1
PIECE = 256
RING = 3
RAW, SPLIT = 6, 4
CHUNK = 4096
UNIT = CHUNK // 2

ROWS = {}
_at = 0
for _name, _n in (("conv_w", TAPS * CT), ("conv_b", CT), ("ba", 2 * CT), ("bx", 2 * CT), ("lam", 2 * CT),
                  ("sc_w", CTAPS * CT), ("g1n", KT), ("ada_b", 2 * KT)):
    ROWS[_name] = (_at, _n)
    _at += _n
NROWS = _at


def order(text):
    steps = []
    for word in text.split():
        name = word.rstrip("0123456789")
        steps.append((name, int(word[len(name):])))
    return steps


PE_ORDER = order("""
    main0 main1 gi0 gr0 gi1 main2 gr1 main3 gi2 gr2 gi3 main4 gr3 main5 gi4 gr4 gi5 main6 gr5 main7 gi6 gr6 gi7 main8 gr7
    main9""")
ACT_ORDER = order("""
    post0 split2 post1 split3 si0 sr0 te0 si1 root0 sr1 te1 post2 split4 root1 si2 sr2 te2 post3 split5 si3 root2 yhi0
    sr3 te3 post4 split6 root3 si4 sr4 te4 post5 split7 si5 root4 yhi1 sr5 te5 post6 split8 root5 si6 sr6 te6 post7 split9
    si7 root6 yhi2 sr7 te7 post8 split10 root7 post9 split11 yhi3 split12 split13 yhi4 split14 yhi5 split15 post14
    split16 post15 split17 split18 split19 yhi6 wo0 wo1 wo2 yhi7 wo3""")
DVE_ORDER = order("""
    cva0 cvb0 ix0 sq0 ix1 sc0 cva1 sq1 cvb1 sc1 yrnn0 ix2 sq2 ix3 sc2 cva2 sq3 cvb2 sc3 yrnn1 ix4 ada0 sq4 ix5 sc4 cva3
    sq5 cvb3 sc5 yrnn2 ix6 ada1 sq6 ix7 sc6 ada2 sq7 sc7 yrnn3 v10 ada3 v11 ada4 ada5 b12 row0 row1 ada6 b13 row2 row3
    ada7 ada8 row4 row5 ada9 ada10 row6 row7 ada11 v16 row8 row9 ada12 v17 row10 row11 ada13 ada14 b18
    row12 row13 ada15 wo0 wo1 b19 row14 row15 wo2 wo3""")


class Own:

    def __init__(self, eng, sem):
        self.eng, self.sem, self.n = eng, sem, 0

    def did(self, instruction):
        instruction.then_inc(self.sem, 1)
        self.n = self.n + 1

    def wait(self, behind=0):
        if self.n > behind:
            self.eng.wait_ge(self.sem, self.n - behind)


class Block:

    def __init__(self, n, half, par):
        self.n, self.half, self.par = n, half, par


class Chunk:

    def __init__(self, n, slot, turn):
        self.n, self.slot, self.turn = n, slot, turn


def layer(nc, A, out):
    ctx = ExitStack()
    with ctx:
        def sem(name):
            return ctx.enter_context(nc.semaphore(name))

        top = {"at": (nc.sbuf_base + 63) // 64 * 64}

        def place(name, shape, dt, at):
            return nc.alloc_sbuf_tensor_at(name, shape, dt, offset=at)

        def const(name, shape, dt=F32):
            n = int(np.prod(shape[1:])) * 4
            t = place(name, shape, dt, top["at"])
            top["at"] += (n + 31) // 32 * 32
            return t

        K = 1024
        ident = const("ident", [P, P])
        ones = const("ones", [P, P])
        tri = const("tri", [P, P])
        iota = const("iota", [P, P])
        prm = const("prm", [P, P])
        c_rows = const("c_rows", [2 * KT, P])
        c_cols = const("c_cols", [P, 2 * KT])
        prmT = const("prmT", [P, NROWS])
        silu_c = const("silu_c", [P, 2 * KT])
        mod_a = const("mod_a", [P, 2, KT])
        mod_s = const("mod_s", [P, 2, KT])
        q8 = const("q8", [P, 2 * CT])
        nq8 = const("nq8", [P, 2 * CT])
        spt = const("spt", [P, 5, 2 * CT])
        ssq = const("ssq", [P, 16])
        std = const("std", [P, 16])
        rstd = const("rstd", [P, 16])
        w_route = const("w_route", [P, KT, NG + NE])
        b_route = const("b_route", [NG + NE, 1])
        odd_sum = const("odd_sum", [P, PIECE])
        eps = const("eps", [P, 1])
        marks = const("marks", [P, 4])
        ones_e = const("ones_e", [P, NE])
        tok_id = const("tok_id", [P, TOPK, NT])
        tok_tab = const("tok_tab", [P, NB + 1], I32)
        id_tab = const("id_tab", [P, NB + 1], I32)
        gate_tab = const("gate_tab", [P, NB])
        ovf_exp = const("ovf_exp", [P, NOVF], I32)
        n_ovf = const("n_ovf", [P, 1], I32)
        lo_end = const("lo_end", [P, 1], I32)
        tok_now = [const(f"tok_now{i}", [P, 1], I32) for i in range(2)]
        id_now = [const(f"id_now{i}", [P, 1], I32) for i in range(2)]
        gate_now = [const(f"gate_now{i}", [P, 1]) for i in range(2)]
        aH = (top["at"] + 63) // 64 * 64
        aY = aH + 80 * K
        aT = aY + 64 * K
        aWR = aT + 16 * K
        aWS = aWR + 24 * K
        assert aWS + 16 * K <= nc.sbuf_usable_end, (aWS + 16 * K, nc.sbuf_usable_end)

        h_hi = place("h_hi", [P, KT, SEQ], F32R, aH)
        h_lo = place("h_lo", [P, KT, SEQ], F32R, aH + 32 * K)
        hc_hi = place("hc_hi", [P, KT, CTX], F32R, aH + 64 * K)
        hc_lo = place("hc_lo", [P, KT, CTX], F32R, aH + 72 * K)
        x_all = place("x_all", [P, NTC, D], F32, aY)
        h_tmp = place("h_tmp", [P, 2, 512], F32, aT)
        squared = place("squared", [P, D], F32, aT + 8 * K)
        mod_row = place("mod_row", [2, 2, PIECE], F32, aT + 12 * K)
        piece = [place(f"piece{i}", [P, KT, PIECE], F32, aWR + 8 * K * i) for i in range(RING)]
        ws_hi = [place(f"ws_hi{i}", [P, KT, P], F32R, aWS + 8 * K * i) for i in range(2)]
        ws_lo = [place(f"ws_lo{i}", [P, KT, P], F32R, aWS + 8 * K * i + 4 * K) for i in range(2)]
        y_hi = [place(f"y_hi{i}", [P, SEQ], F32R, aY + 4 * K * i + (16 * K if i >= 4 else 0)) for i in range(8)]
        y_lo = [place(f"y_lo{i}", [P, SEQ], F32R, aY + 16 * K + 4 * K * i + (16 * K if i >= 4 else 0)) for i in range(8)]
        aR = aY + 32 * K
        gate_w = place("gate_w", [P, CT, 4, P], F32, aR)
        r_at = aR + 8 * K
        step = (XR * 4 + 31) // 32 * 32
        xr_pad = place("xr_pad", [P, XR], F32, r_at)
        xc = place("xc", [P, XC], F32, r_at + step)
        r_a = place("r_a", [P, XC], F32, r_at + 2 * step)
        t_s = place("t_s", [P, XC], F32, r_at + 3 * step)
        v_s = place("v_s", [P, XC], F32, r_at + 4 * step)
        turn_buf = [r_a, t_s, v_s]
        i_h = [place(f"i_h{d}", [P, XC], F32, r_at + (5 + d) * step) for d in range(2)]
        r_end = r_at + 7 * step
        assert r_end <= aT + 12 * K
        gelu_g = [place("gelu_g0", [P, SEQ], F32, aY + 12 * K), place("gelu_g1", [P, SEQ], F32, aY + 28 * K)]
        conv_u = [place(f"conv_u{i}", [P, SEQ], F32, aT + 12 * K * (1 - i)) for i in range(2)]
        conv_y = [place(f"conv_y{i}", [P, SEQ], F32, aT + 4 * K + 4 * K * i) for i in range(2)]
        wo_hi = place("wo_hi", [P, KT, D], F32R, aH)
        wo_lo = place("wo_lo", [P, KT, D], F32R, aH + 32 * K)
        rows = place("rows", [P, 4, D], F32, aH + 64 * K)
        x_in = [place(f"x_in{i}", [P, D], F32, aWS + 8 * K * i) for i in range(2)]
        x1 = [place(f"x1_{i}", [P, D], F32, aWS + 8 * K * i + 4 * K) for i in range(2)]
        norm2 = place("norm2", [P, D], F32, aT + 4 * K)
        m_row = [place(f"m_row{i}", [P, D], F32, aT + 4 * K * i) for i in range(2)]
        mT = [place(f"mT{i}", [P, KT, P], F32, aT + 8 * K + 4 * K * i) for i in range(2)]
        logitT = place("logitT", [NG + NE, NT, P], F32, aWR + 16 * K)
        slot_hot = place("slot_hot", [P, TOPK * NT, P], F32, aWR + 16 * K)
        rt = {"at": aWS}

        def tmp(name, shape, dt=F32):
            t = place(name, shape, dt, rt["at"])
            rt["at"] += (int(np.prod(shape[1:])) * 4 + 31) // 32 * 32
            assert rt["at"] <= aWS + 16 * K
            return t

        logit = tmp("logit", [P, NT, NG + NE])
        g_pad = tmp("g_pad", [P, NT, 8])
        g_top = tmp("g_top", [P, NT, 8])
        g_idx = tmp("g_idx", [P, NT, 8], U32)
        e8 = tmp("e8", [P, NT, 8])
        e_top = tmp("e_top", [P, NT, 8])
        e_idx = tmp("e_idx", [P, NT, 8], U32)
        gi = tmp("gi", [P, NT])
        g_hot = tmp("g_hot", [P, NT, NG])
        xs = tmp("xs", [P, NT, 14])
        xe = tmp("xe", [P, NT, 14])
        dens = tmp("dens", [P, 4, NT])
        gates = tmp("gates", [P, TOPK, NT])
        e_k = tmp("e_k", [P, TOPK, NT])
        big = tmp("big", [P, NT, NE])
        four = tmp("four", [P, NT, NE])
        ovf_c = place("ovf_c", [P, NOVF, NE], F32, rt["at"])
        hot = tmp("hot", [P, TOPK, NT, NE])
        hot_s = tmp("hot_s", [P, NT, NE])
        pre = tmp("pre", [P, NT + 1, NE])
        rank = tmp("rank", [P, TOPK, NT])
        rank_i = tmp("rank_i", [P, TOPK, NT], I32)
        bq_i = tmp("bq_i", [P, TOPK, NT], I32)
        s_i = tmp("s_i", [P, TOPK, NT], I32)
        bq = tmp("bq", [P, TOPK, NT])
        s_f = tmp("s_f", [P, TOPK, NT])
        ov_k = tmp("ov_k", [P, TOPK, NT])
        blk_k = tmp("blk_k", [P, TOPK, NT])
        cnt = tmp("cnt", [P, NE])
        cnt_i = tmp("cnt_i", [P, NE], I32)
        extra = tmp("extra", [P, NE])
        incl = tmp("incl", [P, NE])
        excl = tmp("excl", [P, NE])
        ov_f = tmp("ov_f", [P, NOVF])
        slots_f = tmp("slots_f", [P, 2, NB])
        slot_v = tmp("slot_v", [P, NB])
        blk_hot = place("blk_hot", [P, TOPK * NT, 2, NB], F32, aT + 8 * K)
        raw_at = [aWR] + [aH + 16 * K * i for i in range(5)]
        raw = [place(f"raw{i}", [P, CHUNK], F32, raw_at[i]) for i in range(RAW)]
        w_hi = [place(f"w_hi{i}", [P, UNIT], F32R, aY + 16 * K * i) for i in range(SPLIT)]
        w_lo = [place(f"w_lo{i}", [P, UNIT], F32R, aY + 16 * K * i + 8 * K) for i in range(SPLIT)]
        xT_hi = place("xT_hi", [P, KT, P], F32R, aWS)
        xT_lo = place("xT_lo", [P, KT, P], F32R, aWS + 4 * K)
        s_act = place("s_act", [P, FF], F32, aWS + 8 * K)
        h_act = place("h_act", [P, FF], F32, aWS + 10 * K)
        hT_hi = place("hT_hi", [P, FT, P], F32R, aWS + 12 * K)
        hT_lo = place("hT_lo", [P, FT, P], F32R, aWS + 14 * K)
        x_e = [place(f"x_e{i}", [P, D], F32, aT + 4 * K * i) for i in range(2)]
        y_e = [place(f"y_e{i}", [P, D], F32, aT + 8 * K + 4 * K * i) for i in range(2)]
        fin_y = [place(f"fin_y{i}", [P, TOPK, D], F32, aY + 8 * K * i) for i in range(NT)]
        fin_x = [place(f"fin_x{i}", [P, NT // 2, D], F32, raw_at[i]) for i in range(2)]
        fin_rows = place("fin_rows", [P, 2, D], F32, aWR + 16 * K)

        main = ctx.enter_context(nc.psum_tensor("main", [P, 2, 1024], F32))
        lat = ctx.enter_context(nc.psum_tensor("lat", [P, 2, 512], F32))
        b6 = ctx.enter_context(nc.psum_tensor("b6", [P, 512], F32))
        b7 = ctx.enter_context(nc.psum_tensor("b7", [P, 512], F32))

        x1_d = nc.dram_tensor("x1_d", [SEQ, D], F32, kind="Internal").ap()
        m_d = nc.dram_tensor("m_d", [SEQ, D], F32, kind="Internal").ap()
        y_d = nc.dram_tensor("y_d", [TOPK * SEQ, D], F32, kind="Internal").ap()
        g2_d = nc.dram_tensor("g2_d", [1, D], F32, kind="Internal").ap()

        names = """c_in c_turned c_set mv_done mrow_set mrow_turned rstd_set xs0_set params_in x0_in x1_in xc_in
            gate_w_in route_in norm2_in bias_in rows_zero h_used
            act_own dve_own pool_own consts_set gatew_zero params_turned params_set silu_set lam_exp lam_ln lam_w coef_set
            mod_set std_set xs_set turned unit_h unit_hi unit_lo
            m_hi m_lo main_done free0 free1 ctx_free pads_set xc_set gate_done gate_free
            hsum_set is_set tanh_set exp_set s2_set s_set scan_done y_set yhi_set ylo_set u_set
            acc_set bc_done row_set g2_out wo_hi_s wo_lo_s
            x_in0 x_in1 x1_set x1_out0 x1_out1 m_set m_out0 m_out1 mturn_done mT_set logit_done lT_set lback_done slot_set slot_hot_set
            rexp_in rexp_set hot_set cum_done tabs_in tabs_done tabs_set
            ex_tok ex_id ex_gate gath0 gath1 scat0 scat1 tx_done xh_set xl_set silu_e h_set th_done hh_set hl_set
            y_out unit_used hi_done lo_done
            fx0 fx1 frow_in fadd fmul_pool fsum fsq fstd fout out_done moe_done_a moe_done_p""".split()
        S = {n: sem(n) for n in names}
        ring_in = [sem(f"ring_in{i}") for i in range(RING)]
        fin_in = [sem(f"fin_in{i}") for i in range(NT)]
        raw_in = [sem(f"raw_in{i}") for i in range(RAW)]

        ada = A["ada_w"][0].rearrange("(j p) n -> p j n", p=P)
        w_in = A["w_in"][0].rearrange("(j p) n -> p j n", p=P)
        w_out = A["w_out"][0].rearrange("(j p) n -> p j n", p=P)
        N_ADA1 = 2 * D // PIECE
        kinds = [("ada1", i + w * N_ADA1 // 2) for i in range(N_ADA1 // 2) for w in range(2)]
        a2 = 0
        for n, n_a in enumerate((0, 0, 1, 1, 1, 2, 2, 3, 4, 2)):
            kinds.append(("w", n))
            kinds += [("ada2", a2 + i) for i in range(n_a)]
            a2 += n_a
        N_ADA2 = a2
        kinds += [("wo", i) for i in range(4)]
        assert N_ADA2 * PIECE == 4 * D
        piece_no = {k: n for n, k in enumerate(kinds)}
        v0, bgt0, cgt0 = 1024, 1536, 2048
        w_col = [0, 512, PIECE, 512 + PIECE]
        for half in range(2):
            w_col += [cgt0 + PIECE * half, v0 + PIECE * half, bgt0 + PIECE * half]
        what = [("xr", 0), ("xr", 1), ("gr", 0), ("xr", 2), ("gr", 1), ("xr", 3), ("gr", 2), ("gr", 3)]
        tile_piece = [(0, 0), (0, 1), (1, 0), (2, 0), (1, 1), (2, 1), (3, 0), (3, 1)]
        for half in range(2):
            for k in ("cg", "v", "b"):
                what += [(k, 2 * half), (k, 2 * half + 1)]
        N_MAIN = len(what)
        tile_piece += [divmod(n, 2) for n in range(len(tile_piece), N_MAIN)]
        last_tile = {w: max(n for n in range(N_MAIN) if tile_piece[n][0] == w) for w, _ in tile_piece}

        def tile_weights(n):
            w, half = tile_piece[n]
            return piece[piece_no[("w", w)] % RING][:, :, P * half:P * half + P]

        what_index = {w: n for n, w in enumerate(what)}

        def piece_src(kind, i):
            if kind == "ada1":
                return ada[:, :, PIECE * i:PIECE * (i + 1)]
            if kind == "ada2":
                return ada[:, :, 2 * D + PIECE * i:2 * D + PIECE * (i + 1)]
            if kind == "w":
                return w_in[:, :, w_col[i]:w_col[i] + PIECE]
            return w_out[:, 2 * i:2 * i + 2, :]

        def piece_dst(n):
            kind, _ = kinds[n]
            t = piece[n % RING]
            return t[:] if kind != "wo" else t[:].rearrange("p j n -> p (j n)").rearrange("p (j n) -> p j n", j=2)

        def piece_wait(eng, n):
            eng.wait_ge(ring_in[n % RING], 16 * (n // RING + 1))

        def col(name, i):
            at, n = ROWS[name]
            assert i < n
            return prmT[:, at + i:at + i + 1]

        def cols(name):
            at, n = ROWS[name]
            return prmT[:, at:at + n]

        free = [S["free0"], S["free1"]]
        groups = [(0, 4, 0), (4, 4, 0), (8, 2, 1)]
        units = [(g, 2 * k + i) for k in range(KT // 2) for g in range(3) for i in range(2)]

        def bank(u):
            if u >= 18:
                return main[:, 1, 512 * (u % 2):512 * (u % 2) + 512]
            return main[:, (u % 4) // 2, 512 * (u % 2):512 * (u % 2) + 512]

        exp_w = {"g": A["exp_w_gate"].rearrange("l e (p j) n -> (l e) p (j n)", p=P),
                 "u": A["exp_w_up"].rearrange("l e (p j) n -> (l e) p (j n)", p=P),
                 "d": A["exp_w_down"].rearrange("l e (p j) n -> (l e) p (j n)", p=P)}

        def step_plan(i, k):
            b = Block(2 * i + 3 + k, i + (3 + k) // 2, (3 + k) % 2)
            cs = [Chunk(6 * i + 8 + 3 * k + c, (8 + 3 * k + c) % RAW, i + (8 + 3 * k + c) // RAW) for c in range(3)]
            return b, cs

        def plain(b):
            c0 = 3 * b - 1 if b else 0
            return Block(b, b // 2, b % 2), [Chunk(c0 + c, (c0 + c) % RAW, (c0 + c) // RAW) for c in range(3)]

        def before(b):
            return Block(b.n - 1, b.half - 1 + b.par, 1 - b.par)

        def after(b):
            return Block(b.n + 1, b.half + b.par, 1 - b.par)

        LOOPS = (NE - 4) // 2
        LAST = Chunk(3 * NE - 1, (3 * NE - 1) % RAW, (3 * NE - 1) // RAW)

        def pair_plan(i):
            base = 3 * NE
            return [(Block(NE + 2 * i + k, NE // 2 + i, k),
                     [Chunk(base + 6 * i + 3 * k + c, (3 * k + c) % RAW, base // RAW + i) for c in range(3)])
                    for k in range(2)]

        gath, scat = [S["gath0"], S["gath1"]], [S["scat0"], S["scat1"]]

        block = ctx.enter_context(nc.Block())

        @block.sync
        def _(sp):
            def rows_in(name, src):
                at, n = ROWS[name]
                sp.dma_start(prm[at:at + n, :], src).then_inc(S["params_in"], 16)

            sp.dma_start(c_rows[0:KT, :], A["c"][0].rearrange("(c p) -> c p", p=P)).then_inc(S["c_in"], 16)
            sp.dma_start(c_rows[KT:2 * KT, :], A["c_ctx"].rearrange("(c p) -> c p", p=P)).then_inc(S["c_in"], 16)
            x_rows = A["x"][0].rearrange("(t p) d -> p t d", p=P)

            def load_piece(n):
                if n >= RING:
                    kind, m = kinds[n - RING]
                    if kind == "ada1":
                        sp.wait_ge(S["mv_done"], n - RING + 1)
                    elif kind == "ada2":
                        sp.wait_ge(S["acc_set"], m + 1)
                    elif kind == "w":
                        sp.wait_ge(S["m_lo"], last_tile[m] + 1)
                    else:
                        sp.wait_ge(S["wo_lo_s"], m + 1)
                sp.dma_start(piece_dst(n), piece_src(*kinds[n])).then_inc(ring_in[n % RING], 16)

            load_piece(0)
            sp.dma_start(x_all[:, 0:4, :], x_rows[:, 0:4, :]).then_inc(S["x0_in"], 16)
            load_piece(1)
            rows_in("conv_w", A["rnn_conv_w"][0].rearrange("k (c p) -> (k c) p", p=P))
            rows_in("conv_b", A["rnn_conv_b"][0].rearrange("(c p) -> c p", p=P))
            rows_in("ba", A["rg_ba"][0].rearrange("d (c p) -> (d c) p", p=P))
            rows_in("bx", A["rg_bx"][0].rearrange("d (c p) -> (d c) p", p=P))
            rows_in("lam", A["rg_lambda"][0].rearrange("d (c p) -> (d c) p", p=P))
            rows_in("sc_w", A["sc_conv_w"][0].rearrange("k (c p) -> (k c) p", p=P))
            rows_in("g1n", A["norm1_g"][0].rearrange("(c p) -> c p", p=P))
            rows_in("ada_b", A["ada_b"][0, 0:2 * D].rearrange("(c p) -> c p", p=P))
            sp.dma_start(x_all[:, 4:8, :], x_rows[:, 4:8, :]).then_inc(S["x1_in"], 16)
            load_piece(2)
            sp.dma_start(x_all[:, 8:10, :], A["ctx"][0].rearrange("(t p) d -> p t d", p=P)).then_inc(S["xc_in"], 16)
            for n in range(3, N_ADA1 + 2):
                load_piece(n)
            sp.wait_ge(S["gatew_zero"], 1)
            for d in range(2):
                for kind, src in ((0, A["rg_wa"]), (1, A["rg_wx"])):
                    for e in range(2):
                        dst = gate_w[64 * e:64 * e + 64, :, 2 * d + kind, 64 * e:64 * e + 64]
                        sp.dma_start(dst, src[0, d].rearrange("(c e) i j -> e i c j", e=2)[e]).then_inc(S["gate_w_in"], 16)
            sp.dma_start(w_route[:, :, 0:NG], A["router_group_w"][0].rearrange("(j p) n -> p j n", p=P)).then_inc(S["route_in"], 16)
            sp.dma_start(w_route[:, :, NG:NG + NE], A["router_exp_w"][0].rearrange("(j p) n -> p j n", p=P)).then_inc(S["route_in"], 16)
            sp.dma_start(b_route[0:NG, :], A["router_group_b"].rearrange("a n -> n a")).then_inc(S["route_in"], 16)
            sp.dma_start(b_route[NG:NG + NE, :], A["router_exp_b"].rearrange("a n -> n a")).then_inc(S["route_in"], 16)
            for n in range(N_ADA1 + 2, piece_no[("w", 4)]):
                load_piece(n)
            sp.wait_ge(S["rows_zero"], 1)
            sp.dma_start(rows[0:1, :, :].rearrange("p w n -> p (w n)"), A["ada_b"][:, 2 * D:6 * D]).then_inc(S["bias_in"], 16)
            for n in range(piece_no[("w", 4)], len(kinds)):
                load_piece(n)
            sp.wait_ge(S["ylo_set"], KT)
            sp.dma_start(norm2[:], A["norm2_g"].to_broadcast([P, D])).then_inc(S["norm2_in"], 16)
            x_in_s, x1_out, m_out = [S["x_in0"], S["x_in1"]], [S["x1_out0"], S["x1_out1"]], [S["m_out0"], S["m_out1"]]
            sp.wait_ge(S["main_done"], N_MAIN)
            for t in range(2):
                sp.dma_start(x_in[t][:], A["x"][0, P * t:P * t + P, :]).then_inc(x_in_s[t], 16)
            sp.wait_ge(S["wo_lo_s"], 4)

            def load_chunk(c, which, e, guard):
                if guard:
                    sp.wait_ge(S["lo_done"], 2 * (c.n - RAW) + 2)
                src = exp_w[which]
                src = src[e] if isinstance(e, int) else src[bass.ds(e, 1)].rearrange("a p f -> (a p) f")
                sp.dma_start(raw[c.slot][:], src).then_inc(raw_in[c.slot], 16)

            sp.dma_start(raw[0][:], exp_w["g"][0]).then_inc(raw_in[0], 16)
            sp.wait_ge(S["row_set"], N_ADA2)
            sp.dma_start(g2_d, rows[0:1, 3, :]).then_inc(S["g2_out"], 16)
            sp.wait_ge(S["g2_out"], 16)
            for t in range(NT):
                sp.wait_ge(S["x1_set"], t + 1)
                sp.dma_start(x1_d[P * t:P * t + P, :], x1[t % 2][:]).then_inc(x1_out[t % 2], 16)
                if t + 2 < NT:
                    sp.dma_start(x_in[t % 2][:], A["x"][0, P * (t + 2):P * (t + 3), :]).then_inc(x_in_s[t % 2], 16)
                sp.wait_ge(S["m_set"], t + 1)
                sp.dma_start(m_d[P * t:P * t + P, :], m_row[t % 2][:]).then_inc(m_out[t % 2], 16)
            sp.wait_ge(S["main_done"], N_MAIN + NT)
            first = [("g", 0), ("u", 0), ("g", 1), ("u", 1), ("d", 0), ("g", 2)]
            for c in range(1, RAW):
                sp.dma_start(raw[c][:], exp_w[first[c][0]][first[c][1]]).then_inc(raw_in[c], 16)
            _, cs = plain(2)
            load_chunk(cs[1], "u", 2, True)
            sp.wait_ge(gath[0], 16)
            sp.wait_ge(gath[1], 16)
            load_chunk(cs[2], "d", 1, True)
            sp.wait_ge(S["tabs_done"], 1)
            sp.dma_start(fin_rows[:, 0, :], g2_d.to_broadcast([P, D])).then_inc(S["frow_in"], 16)
            sp.dma_start(fin_rows[:, 1, :], A["final_norm_g"].rearrange("(a n) -> a n", a=1).to_broadcast([P, D])).then_inc(S["frow_in"], 16)
            with sp.Fori(0, LOOPS) as i:
                for k in range(2):
                    _, cs = step_plan(i, k)
                    load_chunk(cs[0], "g", 2 * i + 3 + k, True)
                    load_chunk(cs[1], "u", 2 * i + 3 + k, True)
                    load_chunk(cs[2], "d", 2 * i + 2 + k, True)
            _, cs = plain(NE - 1)
            load_chunk(cs[0], "g", NE - 1, True)
            load_chunk(cs[1], "u", NE - 1, True)
            load_chunk(cs[2], "d", NE - 2, True)
            load_chunk(LAST, "d", NE - 1, True)
            more = sp.value_load(n_ovf[0:1, 0:1], min_val=0, max_val=NOVF)
            with sp.Fori(0, NOVF // 2) as i:
                with sp.If(2 * i < more):
                    for k, (b, cs) in enumerate(pair_plan(i)):
                        e = sp.value_load(ovf_exp[0:1, bass.ds(2 * i + k, 1)], min_val=0, max_val=NE - 1)
                        for c, which in zip(cs, "gud"):
                            load_chunk(c, which, e, True)
                sp.nop()
            first_free = sp.value_load(lo_end[0:1, 0:1], min_val=6 * NE - 2 * RAW + 2, max_val=6 * (NE + NOVF) - 2 * RAW + 2)
            x1_rows = x1_d.rearrange("(a t p) d -> a p t d", a=2, p=P)
            for i in range(2):
                if i:
                    sp.wait_ge(scat[0], 16 * (NE // 2))
                sp.wait_ge(S["lo_done"], first_free + 2 * i)
                sp.dma_start(fin_x[i][:], x1_rows[i]).then_inc(S[f"fx{i}"], 16)
            sp.wait_ge(S["moe_done_a"], 1)
            sp.wait_ge(S["moe_done_p"], 1)
            y_rows = y_d.rearrange("(k t p) d -> t p k d", k=TOPK, p=P)
            out_rows = out[0].rearrange("(t p) d -> t p d", p=P)
            for t in range(NT):
                sp.dma_start(fin_y[t][:], y_rows[t]).then_inc(fin_in[t], 16)
            for t in range(NT):
                sp.wait_ge(S["fout"], t + 1)
                sp.dma_start(out_rows[t], fin_y[t][:, 0, :]).then_inc(S["out_done"], 16)
            sp.wait_ge(S["out_done"], 16 * NT)

        @block.gpsimd
        def _(pool):
            own = Own(pool, S["pool_own"])
            own.did(pool.memset(ident[:], 0.0))
            own.did(pool.memset(ones[:], 1.0))
            own.did(pool.memset(tri[:], 1.0))
            own.wait()
            own.did(pool.affine_select(out=ident[:], in_=ident[:], compare_op=ALU.not_equal, fill=1.0, base=0,
                                       pattern=[[-1, P]], channel_multiplier=1))
            own.did(pool.affine_select(out=tri[:], in_=tri[:], compare_op=ALU.is_gt, fill=0.0, base=0,
                                       pattern=[[1, P]], channel_multiplier=-1))
            own.did(pool.iota(iota[:], [[1, P]], base=0, channel_multiplier=0, allow_small_or_imprecise_dtypes=True))
            own.did(pool.iota(tok_id[:].rearrange("p k t -> p (k t)"), [[P, TOPK * NT]], base=1, channel_multiplier=1,
                              allow_small_or_imprecise_dtypes=True))
            own.wait()
            pool.memset(ones_e[:], 1.0).then_inc(S["consts_set"], 1)
            def low(n):
                pool.wait_ge(S["m_hi"], n + 1)
                pool.tensor_tensor(ws_lo[n % 2][:], tile_weights(n), ws_hi[n % 2][:], ALU.subtract).then_inc(S["m_lo"], 1)

            def y_low(tile):
                pool.wait_ge(S["yhi_set"], tile + 1)
                src = gelu_g[tile % 2] if tile < CT else conv_y[tile % 2]
                pool.tensor_tensor(y_lo[tile][:], src[:], y_hi[tile][:], ALU.subtract).then_inc(S["ylo_set"], 1)

            low(0)
            pool.wait_ge(S["turned"], len(units))
            pool.memset(gate_w[:], 0.0).then_inc(S["gatew_zero"], 1)
            pool.wait_ge(S["unit_lo"], len(units))
            pool.memset(xr_pad[:], 0.0).then_inc(S["pads_set"], 1)
            for t in (r_a, t_s, v_s, i_h[0], i_h[1]):
                pool.memset(t[:, CTX:LAT], 0.0).then_inc(S["pads_set"], 1)
            low(1)
            for name, n in ACT_ORDER:
                if name == "split":
                    low(n)
                    if n == 6:
                        pool.wait_ge(S["main_done"], 6)
                        pool.memset(rows[:], 0.0).then_inc(S["rows_zero"], 1)
                elif name == "yhi":
                    y_low(n)

            def gather(b, first):
                if not first:
                    pool.wait_ge(S["tx_done"], b.n - 1)
                if not (isinstance(b.n, int) and b.n < 2):
                    pool.wait_ge(gath[b.par], 16 * b.half)
                pool.tensor_copy(tok_now[b.par][:], tok_tab[:, bass.ds(b.n + 1, 1)]).then_inc(S["ex_tok"], 1)
                pool.wait_ge(S["tabs_set"], 1)
                pool.wait_ge(S["ex_tok"], b.n + 1)
                pool.indirect_dma_start(out=x_e[b.par][:], out_offset=None, in_=m_d,
                                        in_offset=bass.IndirectOffsetOnAxis(ap=tok_now[b.par][:].bitcast(U32), axis=0),
                                        bounds_check=SEQ - 1, oob_is_err=False).then_inc(gath[b.par], 16)

            def gate_col(b, first):
                if not first:
                    pool.wait_ge(S["y_out"], b.n - 1)
                pool.tensor_copy(gate_now[b.par][:], gate_tab[:, bass.ds(b.n, 1)]).then_inc(S["ex_gate"], 1)

            def scatter(b, first):
                if not first:
                    pool.wait_ge(scat[b.par], 16 * b.half)
                pool.tensor_copy(id_now[b.par][:], id_tab[:, bass.ds(b.n + 1, 1)]).then_inc(S["ex_id"], 1)
                pool.wait_ge(S["tabs_set"], 1)
                pool.wait_ge(S["ex_id"], b.n + 1)
                pool.wait_ge(S["y_out"], b.n + 1)
                pool.indirect_dma_start(out=y_d, out_offset=bass.IndirectOffsetOnAxis(ap=id_now[b.par][:].bitcast(U32), axis=0),
                                        in_=y_e[b.par][:], in_offset=None,
                                        bounds_check=TOPK * SEQ - 1, oob_is_err=False).then_inc(scat[b.par], 16)

            def blk(n):
                return Block(n, n // 2, n % 2)

            def split_low(c, hf):
                k = (2 * c.slot + hf) % SPLIT
                pool.wait_ge(S["hi_done"], 2 * c.n + hf + 1)
                pool.tensor_tensor(w_lo[k][:], raw[c.slot][:, UNIT * hf:UNIT * hf + UNIT], w_hi[k][:], ALU.subtract)\
                    .then_inc(S["lo_done"], 1)

            pool.wait_ge(S["mturn_done"], NT)
            pool.wait_ge(S["m_out0"], 16 * (NT // 2))
            pool.wait_ge(S["m_out1"], 16 * (NT // 2))
            pool.memset(x_e[0][:], 0.0).then_inc(S["pool_own"], 1)
            pool.memset(x_e[1][:], 0.0).then_inc(S["pool_own"], 1)
            own.n = own.n + 2
            _, cs = plain(0)
            split_low(cs[0], 0)
            split_low(cs[0], 1)
            split_low(cs[1], 0)
            pool.wait_ge(S["slot_set"], 1)
            for n in range(TOPK * NT - DVE_HOT):
                k, t = divmod(n, NT)
                pool.tensor_scalar(slot_hot[:, n, :], iota[:], s_f[:, k, t:t + 1], None, ALU.is_equal).then_inc(S["slot_hot_set"], 1)
            own.wait()
            pool.wait_ge(S["tabs_set"], 1)
            gather(blk(0), True)
            gather(blk(1), True)
            gate_col(blk(0), True)
            gather(blk(2), False)
            gate_col(blk(1), True)
            gather(blk(3), False)
            gate_col(blk(2), False)
            gather(blk(4), False)
            gather(blk(5), False)
            scatter(blk(0), True)
            gate_col(blk(3), False)
            scatter(blk(1), True)
            with pool.Fori(0, LOOPS) as i:
                for k in range(2):
                    gather(Block(2 * i + 6 + k, i + 3, k), False)
                    scatter(Block(2 * i + 2 + k, i + 1, k), False)
                    gate_col(Block(2 * i + 4 + k, i + 2, k), False)
            for b in (NE - 2, NE - 1):
                scatter(blk(b), False)
            more = pool.value_load(n_ovf[0:1, 0:1], min_val=0, max_val=NOVF)
            with pool.Fori(0, NOVF // 2) as i:
                with pool.If(2 * i < more):
                    for b, _ in pair_plan(i):
                        gate_col(b, False)
                        gather(Block(b.n + 2, b.half + 1, b.par), False)
                        scatter(b, False)
                    pool.wait_ge(S["tabs_set"], 1)
                    pool.wait_ge(scat[0], 16 * (NE // 2 + 1 + i))
                    pool.wait_ge(scat[1], 16 * (NE // 2 + 1 + i))
                    pool.nop()
                pool.nop()
            pool.wait_ge(scat[0], 16 * (NE // 2))
            pool.wait_ge(scat[1], 16 * (NE // 2))
            pool.wait_ge(gath[0], 16 * (NE // 2 + 1))
            pool.wait_ge(gath[1], 16 * (NE // 2 + 1))
            pool.memset(marks[:, 0:1], 0.0).then_inc(S["moe_done_p"], 1)
            for t in range(NT):
                pool.wait_ge(fin_in[t], 16)
                y = fin_y[t]
                pool.tensor_tensor(y[:, 0, :], y[:, 0, :], y[:, 1, :], ALU.add).then_inc(S["fadd"], 1)
                if t in POOL_G2:
                    pool.wait_ge(S["fadd"], t + 1)
                    pool.wait_ge(S["frow_in"], 32)
                    pool.tensor_tensor(y[:, 0, :], y[:, 0, :], fin_rows[:, 0, :], ALU.mult).then_inc(S["fmul_pool"], 1)

        @block.tensor
        def _(pe):
            def three(out_ap, a, b, first, last):
                pe.matmul(out_ap, a[0], b[0], start=first, stop=False)
                pe.matmul(out_ap, a[0], b[1], start=False, stop=False)
                return pe.matmul(out_ap, a[1], b[0], start=False, stop=last)

            pe.wait_ge(S["consts_set"], 1)
            pe.wait_ge(S["c_in"], 32)
            pe.transpose(lat[:, 0, 0:2 * KT], c_rows[:], ident[0:2 * KT, 0:2 * KT]).then_inc(S["c_turned"], 1)

            def modulation(q):
                piece_wait(pe, q)
                if q >= 2:
                    pe.wait_ge(S["mrow_set"], q - 1)
                for j in range(KT):
                    mm = pe.matmul((b6, b7)[q % 2][0:2, 0:PIECE], silu_c[:, j:2 * KT:KT], piece[q % RING][:, j, :],
                                   start=(j == 0), stop=(j == KT - 1))
                mm.then_inc(S["mv_done"], 1)

            def turn_mod(q):
                pe.wait_ge(S["mrow_set"], q + 1)
                if q >= 2:
                    pe.wait_ge(S["mod_set"], q // 2)
                for h in range(2):
                    at = 2 * (2 * (q % 2) + h)
                    mm = pe.transpose(lat[:, (q // 2) % 2, at:at + 2], mod_row[:, q % 2, P * h:P * h + P], ident[0:2, 0:2])
                mm.then_inc(S["mrow_turned"], 1)

            def turn(u):
                g, j = units[u]
                t0, nt, _ = groups[g]
                pe.wait_ge(S["xs0_set" if g == 0 else "xs_set"], (4, 4, 6)[g])
                if u >= 4:
                    pe.wait_ge(S["unit_h"], u - 1 if u >= 18 else u - 3)
                for t in range(nt):
                    mm = pe.transpose(bank(u)[:, P * t:P * t + P], x_all[:, t0 + t, P * j:P * j + P], ident[:])
                mm.then_inc(S["turned"], 1)

            pe.wait_ge(S["silu_set"], 1)
            modulation(0)
            pe.wait_ge(S["params_in"], 8 * 16)
            pe.transpose(lat[:, 1, 0:NROWS], prm[0:NROWS, :], ident[0:NROWS, 0:NROWS]).then_inc(S["params_turned"], 1)
            modulation(1)
            turn_mod(0)
            turn_mod(1)
            turn(0)
            turn(1)
            modulation(2)
            turn(2)
            turn(3)
            modulation(3)
            turn(4)
            turn(5)
            turn_mod(2)
            turn_mod(3)
            for k in range(1, KT // 2 - 1):
                for u in range(6 * k, 6 * k + 3):
                    turn(u)
                modulation(2 * k + 2)
                for u in range(6 * k + 3, 6 * k + 6):
                    turn(u)
                modulation(2 * k + 3)
                turn_mod(2 * k + 2)
                turn_mod(2 * k + 3)

            def main_tile(n, slot, uses, with_ctx):
                pe.wait_ge(S["m_lo"], n + 1)
                if uses is not None:
                    pe.wait_ge(free[slot], uses)
                w = (ws_hi[slot], ws_lo[slot])
                for j in range(KT):
                    if n == 0:
                        if j >= KT - 2:
                            pe.wait_ge(S["unit_lo"], len(units))
                        else:
                            turn(6 * 3 + j)
                            pe.wait_ge(S["unit_lo"], 6 * (j // 2) + 6)
                    for h in range(2):
                        mm = three(main[:, slot, 512 * h:512 * h + 512], (w[0][:, j, :], w[1][:, j, :]),
                                   (h_hi[:, j, 512 * h:512 * h + 512], h_lo[:, j, 512 * h:512 * h + 512]),
                                   j == 0, j == KT - 1)
                    if n == N_MAIN - 1 and j % 2 and j < KT - 1:
                        mm.then_inc(S["h_used"], 1)
                if with_ctx is not None:
                    if with_ctx:
                        pe.wait_ge(S["ctx_free"], with_ctx)
                    for j in range(KT):
                        mm = three(b6[:, 0:CTX], (w[0][:, j, :], w[1][:, j, :]), (hc_hi[:, j, :], hc_lo[:, j, :]),
                                   j == 0, j == KT - 1)
                mm.then_inc(S["main_done"], 1)

            count = {"g": 0}

            def gate(k, kind):
                c, d = divmod(k, 2)
                pe.wait_ge(S["xc_set"], c + 1)
                if k == 0:
                    pe.wait_ge(S["gate_w_in"], 8 * 16)
                w = gate_w[:, c, 2 * d + kind, :]
                for part in range(3):
                    g = count["g"]
                    if g >= 3:
                        pe.wait_ge(S["gate_free"], g - 2)
                    if part < 2:
                        mm = pe.matmul(lat[:, part, :], w, xc[:, LAT + 512 * part:LAT + 512 * part + 512], start=True, stop=True)
                    else:
                        mm = pe.matmul(b7[:, 0:CTX], w, xc[:, 0:CTX], start=True, stop=True)
                    mm.then_inc(S["gate_done"], 1)
                    count["g"] += 1

            xr_seen = 0
            for name, n in PE_ORDER:
                if name == "main":
                    is_xr = what[n][0] == "xr"
                    main_tile(n, n % 2, n // 2 if n >= 2 else None, xr_seen if is_xr else None)
                    xr_seen += is_xr
                else:
                    gate(n, 1 if name == "gi" else 0)

            def row_cast(a):
                pe.wait_ge(S["acc_set"], a + 1)
                if a >= 2:
                    pe.wait_ge(S["row_set"], a - 1)
                if a == 0:
                    pe.wait_ge(S["ctx_free"], CT)
                w, at = divmod(a * PIECE, D)
                o = (b7, b6)[a % 2][:, 0:PIECE]
                pe.matmul(o, ones[:], rows[:, w, at:at + PIECE], start=True, stop=True).then_inc(S["bc_done"], 1)

            for n in range(10, N_MAIN):
                main_tile(n, n % 2, n // 2, None)
                for k in range(2):
                    if n >= 12:
                        row_cast(2 * (n - 12) + k)

            def turn_m(t):
                pe.wait_ge(S["m_set"], t + 1)
                if t:
                    pe.wait_ge(S["mT_set"], t)
                for j in range(KT):
                    mm = pe.transpose(lat[:, j // 4, P * (j % 4):P * (j % 4) + P], m_row[t % 2][:, P * j:P * j + P], ident[:])
                mm.then_inc(S["mturn_done"], 1)

            def logits(t):
                pe.wait_ge(S["mT_set"], t + 1)
                if t == 0:
                    pe.wait_ge(S["route_in"], 64)
                else:
                    pe.wait_ge(S["lT_set"], t)
                for j in range(KT):
                    mm = pe.matmul(b6[0:NG + NE, 0:P], w_route[:, j, :], mT[t % 2][:, j, :], start=(j == 0), stop=(j == KT - 1))
                mm.then_inc(S["logit_done"], 1)

            def logits_back(t):
                pe.wait_ge(S["lT_set"], t + 1)
                pe.transpose(b7[:, (NG + NE) * t:(NG + NE) * (t + 1)], logitT[:, t, :], ident[0:NG + NE, 0:NG + NE])\
                    .then_inc(S["lback_done"], 1)

            for t in range(NT):
                slot = t % 2
                pe.wait_ge(free[slot], (N_MAIN + t) // 2)
                for j in range(KT):
                    if t == 0:
                        pe.wait_ge(S["ylo_set"], j + 1)
                    if t == 0 and j % 2 == 0:
                        pe.wait_ge(S["wo_lo_s"], j // 2 + 1)
                    for h in range(2):
                        mm = three(main[:, slot, 512 * h:512 * h + 512],
                                   (y_hi[j][:, P * t:P * t + P], y_lo[j][:, P * t:P * t + P]),
                                   (wo_hi[:, j, 512 * h:512 * h + 512], wo_lo[:, j, 512 * h:512 * h + 512]),
                                   j == 0, j == KT - 1)
                mm.then_inc(S["main_done"], 1)
                if t >= 1:
                    turn_m(t - 1)
                if t >= 2:
                    logits(t - 2)
                if t >= 3:
                    logits_back(t - 3)
            logits(NT - 2)
            turn_m(NT - 1)
            logits_back(NT - 3)
            logits_back(NT - 2)
            logits(NT - 1)
            logits_back(NT - 1)

            pe.wait_ge(S["hot_set"], 1)
            pe.matmul(b7[:, 0:NT * NE], tri[:], hot_s[:].rearrange("p t e -> p (t e)"), start=True, stop=False)
            pe.matmul(b7[:, 0:NT * NE], ones[:], pre[:, 0:NT, :].rearrange("p t e -> p (t e)"), start=False, stop=True)
            pe.matmul(b6[:, 0:NE], ones[:], pre[:, NT, :], start=True, stop=True).then_inc(S["cum_done"], 1)
            pe.wait_ge(S["tabs_in"], 1)
            pe.wait_ge(S["slot_hot_set"], TOPK * NT - DVE_HOT)
            for n in range(TOPK * NT):
                mm = pe.matmul(b7[:, 0:2 * NB], slot_hot[:, n, :], blk_hot[:, n, :, :].rearrange("p a b -> p (a b)"),
                               start=(n == 0), stop=(n == TOPK * NT - 1))
            mm.then_inc(S["tabs_done"], 1)

            def turn_x(b, first):
                pe.wait_ge(gath[b.par], 16 * b.half + 16)
                if not first:
                    pe.wait_ge(S["xl_set"], b.n)
                for j in range(KT):
                    mm = pe.transpose(main[:, 0, P * j:P * j + P], x_e[b.par][:, j:D:KT], ident[:])
                mm.then_inc(S["tx_done"], 1)

            def product(c, stationary, outs, kt):
                per = kt // 2
                for hf in range(2):
                    k = (2 * c.slot + hf) % SPLIT
                    pe.wait_ge(S["lo_done"], 2 * c.n + hf + 1)
                    for jj in range(per):
                        j = hf * per + jj
                        for n, o in enumerate(outs):
                            at = 512 * (len(outs) * jj + n)
                            mm = three(o, (stationary[0][:, j, :], stationary[1][:, j, :]),
                                       (w_hi[k][:, at:at + 512], w_lo[k][:, at:at + 512]), j == 0, j == kt - 1)
                    mm.then_inc(S["unit_used"], 1)

            def gate_up(which, b, c, first):
                if which == "g":
                    pe.wait_ge(S["xl_set"], b.n + 1)
                if not first:
                    pe.wait_ge(S["silu_e" if which == "g" else "h_set"], b.n)
                product(c, (xT_hi, xT_lo), [lat[:, 0 if which == "g" else 1, :]], KT)

            def turn_h(b, first):
                pe.wait_ge(S["h_set"], b.n + 1)
                if not first:
                    pe.wait_ge(S["hl_set"], b.n)
                for j in range(FT):
                    mm = pe.transpose(b6[:, P * j:P * j + P], h_act[:, j:FF:FT], ident[:])
                mm.then_inc(S["th_done"], 1)

            def down(b, c, first):
                pe.wait_ge(S["hl_set"], b.n + 1)
                if not first:
                    pe.wait_ge(S["y_out"], b.n)
                product(c, (hT_hi, hT_lo), [main[:, 1, 0:512], main[:, 1, 512:1024]], FT)

            def step(b, cs, turn_next=True):
                gate_up("g", b, cs[0], False)
                turn_h(before(b), isinstance(b.n, int) and b.n == 1)
                gate_up("u", b, cs[1], False)
                if turn_next:
                    turn_x(after(b), False)
                down(before(b), cs[2], isinstance(b.n, int) and b.n == 1)

            b, cs = plain(0)
            turn_x(b, True)
            gate_up("g", b, cs[0], True)
            gate_up("u", b, cs[1], True)
            turn_x(after(b), False)
            step(*plain(1))
            step(*plain(2))
            with pe.Fori(0, LOOPS) as i:
                for k in range(2):
                    step(*step_plan(i, k))
            b, cs = plain(NE - 1)
            step(b, cs, False)
            turn_h(b, False)
            down(b, LAST, False)
            more = pe.value_load(n_ovf[0:1, 0:1], min_val=0, max_val=NOVF)
            with pe.Fori(0, NOVF // 2) as i:
                with pe.If(2 * i < more):
                    for b, cs in pair_plan(i):
                        turn_x(b, False)
                        gate_up("g", b, cs[0], False)
                        gate_up("u", b, cs[1], False)
                        turn_h(b, False)
                        down(b, cs[2], False)
                pe.nop()

        @block.scalar
        def _(act):
            own = Own(act, S["act_own"])
            act.wait_ge(S["c_set"], 1)
            act.activation(silu_c[:], c_cols[:], ACT.Silu).then_inc(S["silu_set"], 1)

            def scale_rows(g):
                t0, nt, _ = groups[g]
                act.wait_ge(S["rstd_set"], g + 1)
                for t in range(t0, t0 + nt):
                    act.activation(x_all[:, t, :], x_all[:, t, :], ACT.Copy, scale=rstd[:, t:t + 1]).then_inc(S["xs_set"], 1)

            def squares(g):
                t0, nt, _ = groups[g]
                act.wait_ge(S[("x0_in", "x1_in", "xc_in")[g]], 16)
                for t in range(t0, t0 + nt):
                    own.wait()
                    own.did(act.activation(squared[:], x_all[:, t, :], ACT.Square,
                                           accum_out=ssq[:, t:t + 1]))
                own.wait()
                act.activation(std[:, t0:t0 + nt], ssq[:, t0:t0 + nt], ACT.Sqrt, scale=1.0 / D, bias=eps[:])\
                    .then_inc(S["std_set"], 1)

            def unit(u):
                g, j = units[u]
                t0, nt, is_ctx = groups[g]
                n = P * nt
                dst = hc_hi[:, j, :] if is_ctx else h_hi[:, j, P * t0:P * t0 + n]
                act.wait_ge(S["unit_h"], u + 1)
                act.activation(dst, h_tmp[:, u % 2, 0:n], ACT.Copy).then_inc(S["unit_hi"], 1)

            def split(n):
                piece_wait(act, piece_no[("w", tile_piece[n][0])])
                if n >= 2:
                    act.wait_ge(S["main_done"], n - 1)
                act.activation(ws_hi[n % 2][:], tile_weights(n), ACT.Copy).then_inc(S["m_hi"], 1)

            squares(0)
            squares(1)
            unit(0)
            unit(1)
            scale_rows(1)
            squares(2)
            unit(2)
            unit(3)
            scale_rows(2)
            for u in range(4, 18):
                unit(u)
            split(0)
            for u in range(18, len(units)):
                unit(u)
            split(1)
            act.wait_ge(S["lam_w"], 1)
            act.activation(spt[:, 1, :], spt[:, 0, :], ACT.Exp, scale=-1.0).then_inc(S["lam_exp"], 1)
            act.wait_ge(S["lam_w"], 2)
            act.activation(spt[:, 3, :], spt[:, 2, :], ACT.Ln).then_inc(S["lam_ln"], 1)

            count = {"g": 0}

            def sigmoids(k, kind):
                c, d = divmod(k, 2)
                dst = i_h[d] if kind else turn_buf[k % 3]
                for part in range(3):
                    g = count["g"]
                    act.wait_ge(S["gate_done"], g + 1)
                    src = lat[:, part, :] if part < 2 else b7[:, 0:CTX]
                    to = dst[:, LAT + 512 * part:LAT + 512 * part + 512] if part < 2 else dst[:, 0:CTX]
                    act.activation(to, src, ACT.Sigmoid, bias=col(("ba", "bx")[kind], CT * d + c))\
                        .then_inc(S["gate_free"], 1)
                    count["g"] += 1

            def gate_i(k):
                c, d = divmod(k, 2)
                if c:
                    act.wait_ge(S["y_set" if d else "hsum_set"], c)
                sigmoids(k, 1)

            def gate_r(k):
                if k:
                    act.wait_ge(S["s2_set"], k)
                sigmoids(k, 0)

            def coefs(k):
                c, d = divmod(k, 2)
                a, t = turn_buf[k % 3], turn_buf[(k + 1) % 3]
                act.wait_ge(S["gate_free"], count["g"])
                if k == 0:
                    act.wait_ge(S["coef_set"], 1)
                else:
                    act.wait_ge(S["is_set"], k)
                act.activation(t[:], a[:], ACT.Tanh, scale=q8[:, CT * d + c:CT * d + c + 1]).then_inc(S["tanh_set"], 1)
                act.wait_ge(S["tanh_set"], k + 1)
                act.activation(a[:], a[:], ACT.Exp, scale=nq8[:, CT * d + c:CT * d + c + 1]).then_inc(S["exp_set"], 1)

            def root(k):
                v = turn_buf[(k + 2) % 3]
                act.wait_ge(S["s2_set"], k + 1)
                act.activation(v[:], v[:], ACT.Sqrt).then_inc(S["s_set"], 1)

            def post(n):
                kind, c = what[n]
                act.wait_ge(S["main_done"], n + 1)
                src = main[:, n % 2, :]
                if kind == "xr":
                    act.wait_ge(S["pads_set"], 6)
                    if c:
                        act.wait_ge(S["xc_set"], c)
                    act.activation(xr_pad[:, 2:2 + CTX], b6[:, 0:CTX], ACT.Copy).then_inc(S["ctx_free"], 1)
                    act.activation(xr_pad[:, LAT + 2:LAT + 2 + SEQ], src, ACT.Copy).then_inc(free[n % 2], 1)
                elif kind == "gr":
                    if c >= 2:
                        act.wait_ge(S["ylo_set"], c - 1)
                    act.activation(gelu_g[c % 2][:], src, ACT.Gelu_apprx_tanh).then_inc(free[n % 2], 1)
                elif kind == "cg":
                    if c == 1:
                        act.wait_ge(S["y_set"], CT)
                    elif c >= 2:
                        act.wait_ge(S["u_set"], 3 * (c - 1))
                    act.activation(conv_u[c % 2][:], src, ACT.Copy).then_inc(free[n % 2], 1)

            def y_high(tile):
                act.wait_ge(S["y_set"], tile + 1)
                if tile == CT - 1:
                    act.wait_ge(S["ylo_set"], tile)
                src = gelu_g[tile % 2] if tile < CT else conv_y[tile % 2]
                act.activation(y_hi[tile][:], src[:], ACT.Copy).then_inc(S["yhi_set"], 1)

            def out_high(i):
                piece_wait(act, piece_no[("wo", i)])
                if i < 3:
                    act.wait_ge(S["h_used"], i + 1)
                else:
                    act.wait_ge(S["main_done"], N_MAIN)
                act.activation(wo_hi[:, 2 * i:2 * i + 2, :].rearrange("p j n -> p (j n)"),
                               piece[piece_no[("wo", i)] % RING][:].rearrange("p j n -> p (j n)"), ACT.Copy).then_inc(S["wo_hi_s"], 1)

            run = {"wo": out_high, "split": split, "post": post, "si": gate_i, "sr": gate_r, "te": coefs, "root": root, "yhi": y_high}
            for name, *at in ACT_ORDER:
                run[name](*at)

            def mT_copy(t):
                act.wait_ge(S["mturn_done"], t + 1)
                if t >= 2:
                    act.wait_ge(S["logit_done"], t - 1)
                act.activation(mT[t % 2][:].rearrange("p j n -> p (j n)"), lat[:].rearrange("p a n -> p (a n)"), ACT.Copy)\
                    .then_inc(S["mT_set"], 1)

            def logit_copy(t):
                act.wait_ge(S["logit_done"], t + 1)
                act.activation(logitT[:, t, :], b6[0:NG + NE, 0:P], ACT.Identity, bias=b_route[:]).then_inc(S["lT_set"], 1)

            def hi(c, hf):
                k = (2 * c.slot + hf) % SPLIT
                act.wait_ge(raw_in[c.slot], 16 * c.turn + 16)
                if not (isinstance(c.n, int) and c.n < SPLIT // 2):
                    act.wait_ge(S["unit_used"], 2 * c.n + hf + 1 - SPLIT)
                act.activation(w_hi[k][:], raw[c.slot][:, UNIT * hf:UNIT * hf + UNIT], ACT.Copy).then_inc(S["hi_done"], 1)

            for t in range(NT):
                act.wait_ge(S["x1_set"], t + 1)
                if t >= 2:
                    act.wait_ge((S["m_out0"], S["m_out1"])[t % 2], 16 * (t // 2))
                    act.wait_ge(S["mturn_done"], t - 1)
                act.activation(m_row[t % 2][:], x1[t % 2][:], ACT.Square, accum_out=ssq[:, t:t + 1]).then_inc(S["act_own"], 1)
                own.n += 1
                own.wait()
                act.activation(std[:, t:t + 1], ssq[:, t:t + 1], ACT.Sqrt, scale=1.0 / D, bias=eps[:]).then_inc(S["std_set"], 1)
                if t:
                    mT_copy(t - 1)
                if t >= 2:
                    logit_copy(t - 2)
            _, cs = plain(0)
            logit_copy(NT - 2)
            mT_copy(NT - 1)
            act.wait_ge(S["main_done"], N_MAIN + NT)
            hi(cs[0], 0)
            logit_copy(NT - 1)
            hi(cs[0], 1)
            hi(cs[1], 0)
            hi(cs[1], 1)
            act.wait_ge(S["rexp_in"], 1)
            act.activation(xe[:], xs[:], ACT.Exp).then_inc(S["rexp_set"], 1)

            def x_high(b, first):
                act.wait_ge(S["tx_done"], b.n + 1)
                if not first:
                    act.wait_ge(S["unit_used"], up_units(b))
                act.activation(xT_hi[:].rearrange("p j n -> p (j n)"), main[:, 0, :], ACT.Copy).then_inc(S["xh_set"], 1)

            def silu(b, c_gate, first):
                act.wait_ge(S["unit_used"], 2 * c_gate.n + 2)
                if not first:
                    act.wait_ge(S["h_set"], b.n)
                act.activation(s_act[:], lat[:, 0, :], ACT.Silu).then_inc(S["silu_e"], 1)

            def h_high(b, c_prev_down):
                act.wait_ge(S["th_done"], b.n + 1)
                if c_prev_down is not None:
                    act.wait_ge(S["unit_used"], 2 * c_prev_down + 2)
                act.activation(hT_hi[:].rearrange("p j n -> p (j n)"), b6[:], ACT.Copy).then_inc(S["hh_set"], 1)

            def y_out(b, c_down):
                act.wait_ge(S["unit_used"], 2 * c_down + 2)
                act.wait_ge(S["ex_gate"], b.n + 1)
                if not (isinstance(b.n, int) and b.n < 2):
                    act.wait_ge(scat[b.par], 16 * b.half)
                act.activation(y_e[b.par][:], main[:, 1, :], ACT.Copy, scale=gate_now[b.par][:]).then_inc(S["y_out"], 1)

            def up_units(b):
                return 2 * (3 * (b.n - 1)) + 2 if not (isinstance(b.n, int) and b.n == 1) else 4

            def step(b, cs, last=False):
                n = b.n if isinstance(b.n, int) else 99
                if n >= 1:
                    hi(cs[1], 0)
                if n >= 2:
                    y_out(before(before(b)), cs[0].n - 1)
                if n >= 1:
                    hi(cs[1], 1)
                nxt = plain(1)[1][0]
                if n == 0:
                    hi(nxt, 0)
                silu(b, cs[0], n == 0)
                if n == 0:
                    hi(nxt, 1)
                if n >= 1:
                    h_high(before(b), cs[0].n - 1 if n >= 2 else None)
                    hi(cs[2], 0)
                    hi(cs[2], 1)
                if not last:
                    x_high(after(b), False)
                if not last and n >= 1:
                    nxt = Chunk(cs[2].n + 1, (cs[2].slot + 1) % RAW, cs[2].turn + (cs[2].slot + 1) // RAW)
                    hi(nxt, 0)
                    hi(nxt, 1)

            b, cs = plain(0)
            x_high(b, True)
            step(b, cs)
            step(*plain(1))
            step(*plain(2))
            with act.Fori(0, LOOPS) as i:
                for k in range(2):
                    step(*step_plan(i, k))
            b, cs = plain(NE - 1)
            step(b, cs, True)
            hi(LAST, 0)
            hi(LAST, 1)
            h_high(b, cs[2].n)
            y_out(before(b), cs[2].n)
            y_out(b, LAST.n)
            more = act.value_load(n_ovf[0:1, 0:1], min_val=0, max_val=NOVF)
            with act.Fori(0, NOVF // 2) as i:
                with act.If(2 * i < more):
                    for b, cs in pair_plan(i):
                        act.wait_ge(S["tx_done"], b.n + 1)
                        act.activation(xT_hi[:].rearrange("p j n -> p (j n)"), main[:, 0, :], ACT.Copy).then_inc(S["xh_set"], 1)
                        for c in cs[0:2]:
                            hi(c, 0)
                            hi(c, 1)
                        silu(b, cs[0], False)
                        h_high(b, None)
                        hi(cs[2], 0)
                        hi(cs[2], 1)
                        y_out(b, cs[2].n)
                act.nop()
            act.activation(std[:, 15:16], ssq[:, 0:1], ACT.Copy).then_inc(S["moe_done_a"], 1)
            for t in range(NT):
                act.wait_ge(S["fsum"], t + 1)
                act.activation(fin_y[t][:, 1, :], fin_x[t // 4][:, t % 4, :], ACT.Square, accum_out=ssq[:, t:t + 1]).then_inc(S["fsq"], 1)
                act.wait_ge(S["fsq"], t + 1)
                act.activation(std[:, t:t + 1], ssq[:, t:t + 1], ACT.Sqrt, scale=1.0 / D, bias=eps[:]).then_inc(S["fstd"], 1)

        @block.vector
        def _(dve):
            own = Own(dve, S["dve_own"])

            def tt(o, a, b, op):
                own.did(dve.tensor_tensor(o, a, b, op))

            def ts(o, a, s1, s2, op0, op1=None):
                own.did(dve.tensor_scalar(o, a, s1, s2, op0, op1) if op1 is not None else dve.tensor_scalar(o, a, s1, None, op0))

            own.did(dve.memset(eps[:], EPS))
            dve.wait_ge(S["c_turned"], 1)
            dve.tensor_copy(c_cols[:], lat[:, 0, 0:2 * KT]).then_inc(S["c_set"], 1)

            def mod_rows(q):
                dve.wait_ge(S["mv_done"], q + 1)
                if q >= 2:
                    dve.wait_ge(S["mrow_turned"], q - 1)
                dve.tensor_copy(mod_row[:, q % 2, :], (b6, b7)[q % 2][0:2, 0:PIECE]).then_inc(S["mrow_set"], 1)

            def mod_cols(k):
                dve.wait_ge(S["mrow_turned"], 2 * k + 2)
                js = slice(2 * k, 2 * k + 2)
                mod = lat[:, k % 2, 0:8].rearrange("p (w j s) -> p w s j", w=2, s=2)
                bias = cols("ada_b").rearrange("p (w j) -> p w j", w=2)[:, :, js]
                tt(mod_s[:, :, js], mod[:, 0, :, :], bias[:, 0:1, :].to_broadcast([P, 2, 2]), ALU.add)
                own.did(dve.scalar_tensor_tensor(out=mod_a[:, :, js], in0=mod[:, 1, :, :], scalar=1.0,
                                                 in1=bias[:, 1:2, :].to_broadcast([P, 2, 2]), op0=ALU.add, op1=ALU.add))
                own.wait()
                dve.tensor_tensor(mod_a[:, :, js], mod_a[:, :, js], cols("g1n")[:, js].unsqueeze(1).to_broadcast([P, 2, 2]),
                                  ALU.mult).then_inc(S["mod_set"], 1)
                dve.wait_ge(S["mod_set"], k + 1)

            def roots(g):
                t0, nt, _ = groups[g]
                dve.wait_ge(S["std_set"], g + 1)
                dve.reciprocal(rstd[:, t0:t0 + nt], std[:, t0:t0 + nt]).then_inc(S["rstd_set"], 1)

            def unit_h(u):
                g, j = units[u]
                t0, nt, s = groups[g]
                dve.wait_ge(S["turned"], u + 1)
                if u >= 2:
                    dve.wait_ge(S["unit_lo"], u - 1)
                dve.tensor_scalar(h_tmp[:, u % 2, 0:P * nt], bank(u)[:, 0:P * nt], mod_a[:, s, j:j + 1], mod_s[:, s, j:j + 1],
                                  ALU.mult, ALU.add).then_inc(S["unit_h"], 1)

            def unit_l(u):
                g, j = units[u]
                t0, nt, is_ctx = groups[g]
                n = P * nt
                hi_, lo_ = ((hc_hi[:, j, :], hc_lo[:, j, :]) if is_ctx else
                            (h_hi[:, j, P * t0:P * t0 + n], h_lo[:, j, P * t0:P * t0 + n]))
                dve.wait_ge(S["unit_hi"], u + 1)
                dve.tensor_tensor(lo_, h_tmp[:, u % 2, 0:n], hi_, ALU.subtract).then_inc(S["unit_lo"], 1)

            def unit_run(a, b):
                for u in range(a, b):
                    unit_h(u)
                    if u > a:
                        unit_l(u - 1)
                unit_l(b - 1)

            mod_rows(0)
            dve.wait_ge(S["params_turned"], 1)
            dve.tensor_copy(prmT[:], lat[:, 1, 0:NROWS]).then_inc(S["params_set"], 1)
            dve.wait_ge(S["params_set"], 1)
            roots(0)
            dve.wait_ge(S["rstd_set"], 1)
            for t in range(4):
                dve.tensor_scalar(x_all[:, t, :], x_all[:, t, :], rstd[:, t:t + 1], None, ALU.mult).then_inc(S["xs0_set"], 1)
            mod_rows(1)
            mod_cols(0)
            unit_run(0, 2)
            roots(1)
            mod_rows(2)
            unit_run(2, 4)
            roots(2)
            mod_rows(3)
            unit_run(4, 6)
            mod_cols(1)
            unit_run(6, 9)
            mod_rows(4)
            unit_run(9, 12)
            mod_rows(5)
            mod_cols(2)
            unit_run(12, 15)
            mod_rows(6)
            unit_run(15, 18)
            mod_rows(7)
            mod_cols(3)
            unit_run(18, 24)
            lam = cols("lam")
            own.did(dve.tensor_scalar(spt[:, 4, :], lam, -1.0, None, ALU.mult))
            own.wait()
            dve.tensor_tensor(spt[:, 0, :], lam, spt[:, 4, :], ALU.max).then_inc(S["lam_w"], 1)
            dve.wait_ge(S["lam_exp"], 1)
            dve.tensor_scalar(spt[:, 2, :], spt[:, 1, :], 1.0, None, ALU.add).then_inc(S["lam_w"], 1)
            dve.wait_ge(S["lam_w"], 2)
            ts(spt[:, 0, :], spt[:, 2, :], -1.0, None, ALU.add)
            dve.wait_ge(S["lam_ln"], 1)
            own.wait()
            ts(spt[:, 2, :], spt[:, 0, :], 0.0, None, ALU.is_equal)
            own.wait()
            tt(spt[:, 0, :], spt[:, 0, :], spt[:, 2, :], ALU.add)
            tt(spt[:, 3, :], spt[:, 3, :], spt[:, 2, :], ALU.add)
            own.wait()
            own.did(dve.reciprocal(spt[:, 0, :], spt[:, 0, :]))
            tt(spt[:, 3, :], spt[:, 3, :], spt[:, 1, :], ALU.mult)
            own.wait()
            tt(spt[:, 3, :], spt[:, 3, :], spt[:, 0, :], ALU.mult)
            ts(spt[:, 4, :], spt[:, 4, :], 0.0, None, ALU.max)
            own.wait()
            tt(spt[:, 3, :], spt[:, 3, :], spt[:, 4, :], ALU.add)
            own.wait()
            ts(q8[:], spt[:, 3, :], RG_C, None, ALU.mult)
            dve.tensor_scalar(nq8[:], spt[:, 3, :], -RG_C, None, ALU.mult).then_inc(S["coef_set"], 1)

            def tap(c, k):
                return dve.scalar_tensor_tensor(out=xc[:], in0=xr_pad[:, k:k + XC], scalar=col("conv_w", CT * k + c),
                                                in1=xc[:], op0=ALU.mult, op1=ALU.add)

            def conv_first(c):
                dve.wait_ge(free[what_index[("xr", c)] % 2], what_index[("xr", c)] // 2 + 1)
                if c:
                    dve.wait_ge(S["gate_done"], 12 * c)
                    own.wait()
                own.did(dve.tensor_scalar(xc[:], xr_pad[:, 0:XC], col("conv_w", c), col("conv_b", c), ALU.mult, ALU.add))
                own.wait()
                own.did(tap(c, 1))

            def conv_second(c):
                own.wait()
                own.did(tap(c, 2))
                own.wait()
                tap(c, 3).then_inc(S["xc_set"], 1)

            def one_less(k):
                a, t, v = (turn_buf[(k + n) % 3] for n in range(3))
                dve.wait_ge(S["exp_set"], k + 1)
                if k:
                    dve.wait_ge(S["scan_done"], k)
                tt(v[:], a[:], a[:], ALU.mult)
                own.wait()
                dve.scalar_tensor_tensor(out=v[:], in0=v[:], scalar=1.0, in1=t[:], op0=ALU.add, op1=ALU.mult)\
                    .then_inc(S["s2_set"], 1)

            def i_times_x(k):
                c, d = divmod(k, 2)
                dve.wait_ge(S["gate_free"], 6 * k + 3)
                dve.wait_ge(S["xc_set"], c + 1)
                tt(i_h[d][:], i_h[d][:], xc[:], ALU.mult)

            def scan(k):
                d = k % 2
                a, v, b = turn_buf[k % 3], turn_buf[(k + 2) % 3], i_h[d]
                dve.wait_ge(S["s_set"], k + 1)
                own.wait()
                dve.tensor_tensor(b[:], b[:], v[:], ALU.mult).then_inc(S["is_set"], 1)
                dve.wait_ge(S["is_set"], k + 1)
                if d == 0:
                    own.did(dve.tensor_tensor_scan(b[:, 0:CTX], a[:, 0:CTX], b[:, 0:CTX], 0.0, ALU.mult, ALU.add))
                    own.wait()
                    dve.tensor_tensor_scan(b[:, LAT:XC], a[:, LAT:XC], b[:, LAT:XC], b[:, CTX - 1:CTX], ALU.mult, ALU.add)\
                        .then_inc(S["scan_done"], 1)
                else:
                    own.did(dve.tensor_tensor_scan(b[:, CTX - 1::-1], a[:, CTX - 1::-1], b[:, CTX - 1::-1], 0.0, ALU.mult, ALU.add))
                    own.wait()
                    dve.tensor_tensor_scan(b[:, XC - 1:CTX + 2:-1], a[:, XC - 1:CTX + 2:-1], b[:, XC - 1:CTX + 2:-1], b[:, 0:1],
                                           ALU.mult, ALU.add).then_inc(S["scan_done"], 1)

            def y_rnn(c):
                dve.wait_ge(S["scan_done"], 2 * c + 2)
                n = what_index[("gr", c)]
                dve.wait_ge(free[n % 2], n // 2 + 1)
                h, g = i_h[1][:, LAT:XC], gelu_g[c % 2]
                dve.tensor_tensor(h, i_h[0][:, LAT:XC], h, ALU.add).then_inc(S["hsum_set"], 1)
                dve.wait_ge(S["hsum_set"], c + 1)
                dve.tensor_tensor(g[:], h, g[:], ALU.mult).then_inc(S["y_set"], 1)

            def conv_v(n):
                _, c = what[n]
                cg = what_index[("cg", c)]
                dve.wait_ge(S["main_done"], n + 1)
                dve.wait_ge(free[cg % 2], cg // 2 + 1)
                u, y = conv_u[c % 2], conv_y[c % 2]
                dve.wait_ge(S["y_set"], CT)
                if c >= 2:
                    dve.wait_ge(S["ylo_set"], CT + c - 1)
                dve.tensor_tensor(u[:], main[:, n % 2, :], u[:], ALU.mult).then_inc(free[n % 2], 1)
                dve.wait_ge(free[n % 2], n // 2 + 1)
                dve.tensor_scalar(y[:], u[:], col("sc_w", CT + c), None, ALU.mult).then_inc(S["u_set"], 1)
                dve.wait_ge(S["u_set"], 3 * c + 1)
                if c < CT // 2:
                    ug, yg = (t[:].rearrange("p (r w) -> p r w", w=GRID_W) for t in (u, y))
                    sh = [(yg[:, :, 1:GRID_W], ug[:, :, 0:GRID_W - 1]), (yg[:, :, 0:GRID_W - 1], ug[:, :, 1:GRID_W])]
                else:
                    sh = [(y[:, GRID_W:SEQ], u[:, 0:SEQ - GRID_W]), (y[:, 0:SEQ - GRID_W], u[:, GRID_W:SEQ])]
                for k, (o, i) in enumerate(sh):
                    dve.scalar_tensor_tensor(out=o, in0=i, scalar=col("sc_w", 2 * k * CT + c), in1=o, op0=ALU.mult, op1=ALU.add)\
                        .then_inc(S["u_set"], 1)
                    dve.wait_ge(S["u_set"], 3 * c + 2 + k)

            def conv_b(n):
                _, c = what[n]
                dve.wait_ge(S["main_done"], n + 1)
                y = conv_y[c % 2]
                dve.tensor_tensor(y[:], main[:, n % 2, :], y[:], ALU.mult).then_inc(free[n % 2], 1)
                dve.wait_ge(free[n % 2], n // 2 + 1)
                dve.memset(marks[:, 2:3], 0.0).then_inc(S["y_set"], 1)
                dve.wait_ge(S["y_set"], CT + c + 1)

            def ada2(a):
                pn = piece_no[("ada2", a)]
                piece_wait(dve, pn)
                if a == 0:
                    dve.wait_ge(S["bias_in"], 16)
                w, at = divmod(a * PIECE, D)
                o = rows[:, w, at:at + PIECE]
                own.wait()
                for j in range(KT):
                    src = piece[pn % RING][:, j, :]
                    if j >= 2:
                        own.wait(1)
                    if j == 1:
                        own.did(dve.tensor_scalar(odd_sum[:], src, silu_c[:, j:j + 1], None, ALU.mult))
                    else:
                        acc = odd_sum[:] if j % 2 else o
                        own.did(dve.scalar_tensor_tensor(out=acc, in0=src, scalar=silu_c[:, j:j + 1], in1=acc,
                                                         op0=ALU.mult, op1=ALU.add))
                own.wait()
                dve.tensor_tensor(o, o, odd_sum[:], ALU.add).then_inc(S["acc_set"], 1)
                dve.wait_ge(S["acc_set"], a + 1)

            def row_out(a):
                dve.wait_ge(S["bc_done"], a + 1)
                w, at = divmod(a * PIECE, D)
                dve.tensor_copy(rows[:, w, at:at + PIECE], (b7, b6)[a % 2][:, 0:PIECE]).then_inc(S["row_set"], 1)

            def out_low(i):
                dve.wait_ge(S["wo_hi_s"], i + 1)
                dve.tensor_tensor(wo_lo[:, 2 * i:2 * i + 2, :].rearrange("p j n -> p (j n)"),
                                  piece[piece_no[("wo", i)] % RING][:].rearrange("p j n -> p (j n)"),
                                  wo_hi[:, 2 * i:2 * i + 2, :].rearrange("p j n -> p (j n)"), ALU.subtract).then_inc(S["wo_lo_s"], 1)

            run = {"wo": out_low, "cva": conv_first, "cvb": conv_second, "sq": one_less, "ix": i_times_x, "sc": scan, "yrnn": y_rnn, "v": conv_v, "b": conv_b,
                   "ada": ada2, "row": row_out}
            for name, *at in DVE_ORDER:
                run[name](*at)
            dve.wait_ge(S["norm2_in"], 16)
            dve.wait_ge(S["row_set"], N_ADA2)
            own.did(dve.scalar_tensor_tensor(out=rows[:, 2, :], in0=rows[:, 2, :], scalar=1.0, in1=norm2[:], op0=ALU.add, op1=ALU.mult))
            own.wait()

            for t in range(NT):
                par = t % 2
                dve.wait_ge(S["main_done"], N_MAIN + t + 1)
                dve.wait_ge((S["x_in0"], S["x_in1"])[par], 16 * (t // 2) + 16)
                dve.wait_ge(S["row_set"], N_ADA2)
                if t >= 2:
                    dve.wait_ge((S["x1_out0"], S["x1_out1"])[par], 16 * (t // 2))
                dve.tensor_tensor(x1[par][:], main[:, par, :], rows[:, 0, :], ALU.mult).then_inc(free[par], 1)
                dve.wait_ge(free[par], (N_MAIN + t) // 2 + 1)
                dve.tensor_tensor(x1[par][:], x1[par][:], x_in[par][:], ALU.add).then_inc(S["x1_set"], 1)
                dve.wait_ge(S["std_set"], 3 + t + 1)
                own.did(dve.reciprocal(rstd[:, t:t + 1], std[:, t:t + 1]))
                own.wait()
                own.did(dve.scalar_tensor_tensor(out=m_row[par][:], in0=x1[par][:], scalar=rstd[:, t:t + 1], in1=rows[:, 2, :],
                                                 op0=ALU.mult, op1=ALU.mult))
                own.wait()
                dve.tensor_tensor(m_row[par][:], m_row[par][:], rows[:, 1, :], ALU.add).then_inc(S["m_set"], 1)

            def lo(c, hf):
                k = (2 * c.slot + hf) % SPLIT
                dve.wait_ge(S["hi_done"], 2 * c.n + hf + 1)
                dve.tensor_tensor(w_lo[k][:], raw[c.slot][:, UNIT * hf:UNIT * hf + UNIT], w_hi[k][:], ALU.subtract)\
                    .then_inc(S["lo_done"], 1)

            def bc(ap, shape):
                return ap.to_broadcast(shape)

            dve.wait_ge(S["x1_out0"], 16 * (NT // 2))
            dve.wait_ge(S["x1_out1"], 16 * (NT // 2))
            own.did(dve.memset(g_pad[:], -3.0e38))
            own.did(dve.memset(pre[:, 0, :], 0.0))
            dve.wait_ge(S["lback_done"], NT)
            own.did(dve.tensor_copy(logit[:].rearrange("p t n -> p (t n)"), b7[:, 0:NT * (NG + NE)]))
            own.wait()
            own.did(dve.tensor_copy(g_pad[:, :, 0:NG], logit[:, :, 0:NG]))
            own.wait()
            for t in range(NT):
                own.did(dve.max(g_top[:, t, :], g_pad[:, t, :]))
            own.wait()
            for t in range(NT):
                own.did(dve.max_index(g_idx[:, t, :], g_top[:, t, :], g_pad[:, t, :]))
            own.wait()
            own.did(dve.tensor_copy(gi[:], g_idx[:, :, 0]))
            tt(xs[:, :, 0:NG], logit[:, :, 0:NG], bc(g_top[:, :, 0:1], [P, NT, NG]), ALU.subtract)
            own.wait()
            tt(g_hot[:], iota[:, 0:NG].unsqueeze(1).to_broadcast([P, NT, NG]), gi[:].unsqueeze(2).to_broadcast([P, NT, NG]), ALU.is_equal)
            own.wait()
            tt(big[:].rearrange("p t (g e) -> p t g e", g=NG), logit[:, :, NG:NG + NE].rearrange("p t (g e) -> p t g e", g=NG),
               g_hot[:].unsqueeze(3).to_broadcast([P, NT, NG, EPG]), ALU.mult)
            own.wait()
            own.did(dve.tensor_reduce(e8[:], big[:].rearrange("p t (g e) -> p t e g", g=NG), AX, ALU.add))
            own.wait()
            for t in range(NT):
                own.did(dve.max(e_top[:, t, :], e8[:, t, :]))
            own.wait()
            for t in range(NT):
                own.did(dve.max_index(e_idx[:, t, :], e_top[:, t, :], e8[:, t, :]))
            tt(xs[:, :, NG:NG + EPG], e8[:], bc(e_top[:, :, 0:1], [P, NT, EPG]), ALU.subtract)
            own.wait()
            dve.tensor_tensor(xs[:, :, 12:14], e_top[:, :, 0:2], bc(e_top[:, :, 0:1], [P, NT, 2]), ALU.subtract).then_inc(S["rexp_in"], 1)
            for k in range(TOPK):
                own.did(dve.tensor_copy(e_k[:, k, :], e_idx[:, :, k]))
            own.wait()
            for k in range(TOPK):
                own.did(dve.scalar_tensor_tensor(out=e_k[:, k, :], in0=gi[:], scalar=float(EPG), in1=e_k[:, k, :],
                                                 op0=ALU.mult, op1=ALU.add))
            own.wait()
            for k in range(TOPK):
                tt(hot[:, k, :, :], iota[:, 0:NE].unsqueeze(1).to_broadcast([P, NT, NE]),
                   e_k[:, k, :].unsqueeze(2).to_broadcast([P, NT, NE]), ALU.is_equal)
            own.wait()
            tt(hot_s[:], hot[:, 0, :, :], hot[:, 1, :, :], ALU.add)
            own.wait()
            tt(big[:, 1:, :], hot_s[:, 1:, :], hot_s[:, :NT - 1, :], ALU.add)
            own.did(dve.tensor_copy(big[:, 0, :], hot_s[:, 0, :]))
            own.wait()
            tt(four[:, 2:, :], big[:, 2:, :], big[:, :NT - 2, :], ALU.add)
            own.did(dve.tensor_copy(four[:, 0:2, :], big[:, 0:2, :]))
            own.wait()
            own.did(dve.tensor_copy(pre[:, 1:5, :], four[:, 0:4, :]))
            tt(pre[:, 5:, :], four[:, 4:, :], four[:, :NT - 4, :], ALU.add)
            own.wait()
            dve.memset(marks[:, 1:2], 0.0).then_inc(S["hot_set"], 1)
            dve.wait_ge(S["rexp_set"], 1)
            own.did(dve.tensor_reduce(dens[:, 0, :], xe[:, :, 0:NG], AX, ALU.add))
            own.did(dve.tensor_reduce(dens[:, 1, :], xe[:, :, NG:NG + EPG], AX, ALU.add))
            own.wait()
            own.did(dve.reciprocal(dens[:, 0:2, :], dens[:, 0:2, :]))
            own.wait()
            for k in range(TOPK):
                tt(gates[:, k, :], xe[:, :, 12 + k], dens[:, 1, :], ALU.mult)
            own.wait()
            tt(dens[:, 2, :], gates[:, 0, :], gates[:, 1, :], ALU.add)
            own.wait()
            own.did(dve.reciprocal(dens[:, 2, :], dens[:, 2, :]))
            own.wait()
            tt(dens[:, 3, :], dens[:, 0, :], dens[:, 2, :], ALU.mult)
            own.wait()
            for k in range(TOPK):
                tt(gates[:, k, :], gates[:, k, :], dens[:, 3, :], ALU.mult)
            dve.wait_ge(S["cum_done"], 1)
            for k in range(TOPK):
                own.wait()
                tt(big[:], hot[:, k, :, :], b7[:, 0:NT * NE].rearrange("p (t e) -> p t e", t=NT), ALU.mult)
                own.wait()
                own.did(dve.tensor_reduce(rank[:, k, :], big[:], AX, ALU.add))
            ts(cnt[:], b6[:, 0:NE], -1.0, 0.0, ALU.add, ALU.max)
            own.wait()
            own.did(dve.tensor_copy(cnt_i[:], cnt[:]))
            own.did(dve.tensor_copy(rank_i[:], rank[:]))
            own.wait()
            ts(cnt_i[:], cnt_i[:], 7, None, ALU.logical_shift_right)
            ts(bq_i[:], rank_i[:], 7, None, ALU.logical_shift_right)
            ts(s_i[:], rank_i[:], P - 1, None, ALU.bitwise_and)
            own.wait()
            dve.tensor_copy(s_f[:], s_i[:]).then_inc(S["slot_set"], 1)
            own.did(dve.tensor_copy(extra[:], cnt_i[:]))
            own.did(dve.tensor_copy(bq[:], bq_i[:]))
            own.wait()
            own.did(dve.tensor_tensor_scan(incl[:], ones_e[:], extra[:], 0.0, ALU.mult, ALU.add))
            own.wait()
            tt(excl[:], incl[:], extra[:], ALU.subtract)
            for k in range(TOPK):
                own.wait()
                tt(big[:], hot[:, k, :, :], excl[:].unsqueeze(1).to_broadcast([P, NT, NE]), ALU.mult)
                own.wait()
                own.did(dve.tensor_reduce(ov_k[:, k, :], big[:], AX, ALU.add))
            own.wait()
            tt(ov_k[:], ov_k[:], bq[:], ALU.add)
            own.wait()
            tt(ov_k[:], ov_k[:], e_k[:], ALU.subtract)
            ts(blk_k[:], bq[:], 1.0, None, ALU.min)
            own.wait()
            own.did(dve.scalar_tensor_tensor(out=ov_k[:], in0=ov_k[:], scalar=float(NE - 1), in1=blk_k[:], op0=ALU.add, op1=ALU.mult))
            own.wait()
            tt(blk_k[:], e_k[:], ov_k[:], ALU.add)
            own.wait()
            for t in range(NT - DVE_HOT, NT):
                ts(slot_hot[:, NT + t, :], iota[:], s_f[:, 1, t:t + 1], None, ALU.is_equal)
            for k in range(TOPK):
                bh = blk_hot[:, NT * k:NT * k + NT, :, :]
                tt(bh[:, :, 0, :], iota[:, 0:NB].unsqueeze(1).to_broadcast([P, NT, NB]),
                   blk_k[:, k, :].unsqueeze(2).to_broadcast([P, NT, NB]), ALU.is_equal)
            own.wait()
            for k in range(TOPK):
                bh = blk_hot[:, NT * k:NT * k + NT, :, :]
                tt(bh[:, :, 1, :], bh[:, :, 0, :], gates[:, k, :].unsqueeze(2).to_broadcast([P, NT, NB]), ALU.mult)
            own.wait()
            for k in range(TOPK):
                bh = blk_hot[:, NT * k:NT * k + NT, :, :]
                ins = dve.tensor_tensor(bh[:, :, 0, :], bh[:, :, 0, :], tok_id[:, k, :].unsqueeze(2).to_broadcast([P, NT, NB]), ALU.mult)
                if k < TOPK - 1:
                    own.did(ins)
                    own.wait()
                else:
                    ins.then_inc(S["tabs_in"], 1)
            own.did(dve.tensor_copy(n_ovf[:], incl[:, NE - 1:NE]))
            own.did(dve.tensor_copy(lo_end[:], incl[:, NE - 1:NE]))
            tt(ovf_c[:], incl[:].unsqueeze(1).to_broadcast([P, NOVF, NE]), iota[:, 0:NOVF].unsqueeze(2).to_broadcast([P, NOVF, NE]), ALU.is_le)
            own.wait()
            own.did(dve.tensor_reduce(ov_f[:], ovf_c[:], AX, ALU.add))
            own.wait()
            ts(ov_f[:], ov_f[:], float(NE - 1), None, ALU.min)
            own.wait()
            own.did(dve.tensor_copy(ovf_exp[:], ov_f[:]))
            ts(lo_end[:], lo_end[:], 1, None, ALU.add)
            own.wait()
            ts(lo_end[:], lo_end[:], 1, None, ALU.logical_shift_right)
            own.wait()
            ts(lo_end[:], lo_end[:], 12, 6 * NE - 2 * RAW + 2, ALU.mult, ALU.add)
            dve.wait_ge(S["lo_done"], 3)
            lo(plain(0)[1][1], 1)
            dve.wait_ge(S["tabs_done"], 1)
            own.did(dve.tensor_copy(slots_f[:].rearrange("p a b -> p (a b)"), b7[:, 0:2 * NB]))
            own.wait()
            own.did(dve.tensor_copy(gate_tab[:], slots_f[:, 1, :]))
            ts(slot_v[:], slots_f[:, 0, :], 0.0, float(NONE + 1), ALU.is_equal, ALU.mult)
            own.wait()
            own.did(dve.scalar_tensor_tensor(out=slot_v[:], in0=slots_f[:, 0, :], scalar=-1.0, in1=slot_v[:], op0=ALU.add, op1=ALU.add))
            own.wait()
            own.did(dve.tensor_copy(id_tab[:, 1:], slot_v[:]))
            own.wait()
            dve.tensor_scalar(tok_tab[:, 1:], id_tab[:, 1:], NONE + SEQ - 1, None, ALU.bitwise_and).then_inc(S["tabs_set"], 1)

            def x_low(b):
                dve.wait_ge(S["xh_set"], b.n + 1)
                dve.tensor_tensor(xT_lo[:].rearrange("p j n -> p (j n)"), main[:, 0, :], xT_hi[:].rearrange("p j n -> p (j n)"),
                                  ALU.subtract).then_inc(S["xl_set"], 1)

            def h_mul(b, c_up, first):
                dve.wait_ge(S["silu_e"], b.n + 1)
                dve.wait_ge(S["unit_used"], 2 * c_up.n + 2)
                if not first:
                    dve.wait_ge(S["th_done"], b.n)
                dve.tensor_tensor(h_act[:], lat[:, 1, :], s_act[:], ALU.mult).then_inc(S["h_set"], 1)

            def h_low(b):
                dve.wait_ge(S["hh_set"], b.n + 1)
                dve.tensor_tensor(hT_lo[:].rearrange("p j n -> p (j n)"), b6[:], hT_hi[:].rearrange("p j n -> p (j n)"),
                                  ALU.subtract).then_inc(S["hl_set"], 1)

            def step(b, cs, last=False):
                n = b.n if isinstance(b.n, int) else 99
                if n >= 1:
                    lo(cs[1], 0)
                    lo(cs[1], 1)
                    h_low(before(b))
                    lo(cs[2], 0)
                    lo(cs[2], 1)
                if n == 0:
                    nxt = plain(1)[1][0]
                    lo(nxt, 0)
                    lo(nxt, 1)
                h_mul(b, cs[1], n == 0)
                if not last:
                    x_low(after(b))
                if not last and n >= 1:
                    nxt = Chunk(cs[2].n + 1, (cs[2].slot + 1) % RAW, 0)
                    lo(nxt, 0)
                    lo(nxt, 1)

            b, cs = plain(0)
            x_low(b)
            step(b, cs)
            step(*plain(1))
            step(*plain(2))
            with dve.Fori(0, LOOPS) as i:
                for k in range(2):
                    step(*step_plan(i, k))
            b, cs = plain(NE - 1)
            step(b, cs, True)
            lo(LAST, 0)
            lo(LAST, 1)
            h_low(b)
            more = dve.value_load(n_ovf[0:1, 0:1], min_val=0, max_val=NOVF)
            with dve.Fori(0, NOVF // 2) as i:
                with dve.If(2 * i < more):
                    for b, cs in pair_plan(i):
                        x_low(b)
                        for c in cs[0:2]:
                            lo(c, 0)
                            lo(c, 1)
                        h_mul(b, cs[1], False)
                        h_low(b)
                        lo(cs[2], 0)
                        lo(cs[2], 1)
                dve.nop()
            dve.wait_ge(S["frow_in"], 32)
            dve.wait_ge(S["fx0"], 16)
            dve.wait_ge(S["fx1"], 16)

            def norm(t):
                dve.wait_ge(S["fstd"], t + 1)
                own.did(dve.reciprocal(rstd[:, t:t + 1], std[:, t:t + 1]))
                own.wait()
                dve.scalar_tensor_tensor(out=fin_y[t][:, 0, :], in0=fin_x[t // 4][:, t % 4, :], scalar=rstd[:, t:t + 1],
                                         in1=fin_rows[:, 1, :], op0=ALU.mult, op1=ALU.mult).then_inc(S["fout"], 1)

            for t in range(NT):
                y, x = fin_y[t][:, 0, :], fin_x[t // 4][:, t % 4, :]
                if t in POOL_G2:
                    dve.wait_ge(S["fmul_pool"], POOL_G2.index(t) + 1)
                else:
                    dve.wait_ge(S["fadd"], t + 1)
                    tt(y, y, fin_rows[:, 0, :], ALU.mult)
                    own.wait()
                dve.tensor_tensor(x, x, y, ALU.add).then_inc(S["fsum"], 1)
                if t:
                    norm(t - 1)
            norm(NT - 1)


_INS = ["x", "c", "ctx", "c_ctx", "ada_w", "ada_b", "norm1_g", "norm2_g", "w_in", "rnn_conv_w", "rnn_conv_b", "rg_wa",
        "rg_ba", "rg_wx", "rg_bx", "rg_lambda", "sc_conv_w", "w_out", "router_group_w", "router_group_b", "router_exp_w",
        "router_exp_b", "exp_w_gate", "exp_w_up", "exp_w_down", "final_norm_g"]


def kernel(**inputs):
    import concourse.bacc as bacc
    from concourse.bass_utils import run_bass_kernel_spmd

    nc = bacc.Bacc("TRN2", target_bir_lowering=False, num_devices=1)
    arrays, aps = {}, {}
    for name in _INS:
        a = np.ascontiguousarray(inputs[name])
        arrays[f"in_{name}"] = a
        aps[name] = nc.dram_tensor(f"in_{name}", a.shape, mybir.dt.from_np(a.dtype), kind="ExternalInput").ap()
    out = nc.dram_tensor("out_0", (1, SEQ, D), F32, kind="ExternalOutput").ap()
    layer(nc, aps, out)
    r = run_bass_kernel_spmd(nc, [arrays], core_ids=[0])
    return r.results[0]["out_0"]
```
